# Optimizing a Trainium2 kernel written in Bass

```python
import jax, jax.numpy as jnp
from jax import lax
import numpy as np

D_MODEL = 1024
BATCH = 1
SEQ = 1024
DEPTH = 1

N_HEADS_A = 8
HEAD_DIM_A = 64
N_IDX_HEADS = 8
IDX_DIM = 64
TOPK_MAX = 256
Q_BLOCK = 128
N_HEADS_B = 4
HEAD_K_B = 128
HEAD_V_B = 128
CHUNK_B = 64
N_HEADS_C = 4
HEAD_DIM_C = 128
MEM_LEN = 256
N_BRANCH = 3
EPS = 1e-6

WIDTH_A = N_HEADS_A * HEAD_DIM_A
WIDTH_BK = N_HEADS_B * HEAD_K_B
WIDTH_BV = N_HEADS_B * HEAD_V_B
WIDTH_C = N_HEADS_C * HEAD_DIM_C
BRANCH_WIDTH = WIDTH_A
IDX_SCALE = (IDX_DIM ** -0.5) * (N_IDX_HEADS ** -0.5)
IN_SPLITS = (WIDTH_A, WIDTH_A, WIDTH_A, WIDTH_A,
             N_IDX_HEADS * IDX_DIM, IDX_DIM, N_IDX_HEADS,
             WIDTH_BK, WIDTH_BK, WIDTH_BV, WIDTH_BV,
             WIDTH_C, WIDTH_C,
             N_BRANCH * D_MODEL)
N_IN = sum(IN_SPLITS)

kernel_name = "hybrid_dsa_hgrn2_memxattn_gated"

def rms_norm(x, g):
    xf = x.astype(jnp.float32)
    y = xf * lax.rsqrt(jnp.mean(xf * xf, axis=-1, keepdims=True) + EPS)
    return (y * g.astype(jnp.float32)).astype(x.dtype)

def alibi_slopes(n):
    return jnp.exp2(-8.0 * (jnp.arange(n, dtype=jnp.float32) + 1.0) / n)

def dsa_attention(q, k, v, qi, ki, wi):
    B, S = q.shape[0], q.shape[1]
    topk = min(TOPK_MAX, S // 4)
    nb = S // Q_BLOCK
    slopes = alibi_slopes(N_HEADS_A)
    neg = jnp.finfo(jnp.float32).min
    kif = ki.astype(jnp.float32)
    spos = jnp.arange(S, dtype=jnp.int32)

    def to_blocks(a):
        return jnp.swapaxes(a.reshape((B, nb, Q_BLOCK) + a.shape[2:]), 0, 1)

    def block(args):
        qb, qib, wib, start = args
        tpos = start + jnp.arange(Q_BLOCK, dtype=jnp.int32)
        rel = jnp.einsum('bthd,bsd->bths', qib.astype(jnp.float32), kif)
        score = jnp.einsum('bths,bth->bts', jax.nn.relu(rel), wib.astype(jnp.float32)) * IDX_SCALE
        causal = spos[None, :] <= tpos[:, None]
        score = jnp.where(causal[None], score, -jnp.inf)
        _, idx = lax.top_k(score, topk)
        kg = jax.vmap(lambda kk, ii: kk[ii])(k, idx)
        vg = jax.vmap(lambda vv, ii: vv[ii])(v, idx)
        logits = jnp.einsum('bthd,btkhd->bhtk', qb, kg).astype(jnp.float32) * (HEAD_DIM_A ** -0.5)
        dist = (tpos[None, :, None] - idx).astype(jnp.float32)
        logits = logits - slopes[None, :, None, None] * dist[:, None]
        valid = idx <= tpos[None, :, None]
        logits = jnp.where(valid[:, None], logits, neg)
        p = jax.nn.softmax(logits, axis=-1).astype(v.dtype)
        return jnp.einsum('bhtk,btkhd->bthd', p, vg)

    starts = jnp.arange(nb, dtype=jnp.int32) * Q_BLOCK
    o = lax.map(block, (to_blocks(q), to_blocks(qi), to_blocks(wi), starts))
    return jnp.swapaxes(o, 0, 1).reshape(B, S, N_HEADS_A, HEAD_DIM_A)

def hgrn2_recurrence(q, f_pre, i, lb):
    B, S = q.shape[0], q.shape[1]
    n = S // CHUNK_B
    f = lb + (1.0 - lb) * jax.nn.sigmoid(f_pre.astype(jnp.float32))
    logf = jnp.log(f)
    kk = 1.0 - f

    def chunks(a, d):
        return a.astype(jnp.float32).reshape(B, n, CHUNK_B, N_HEADS_B, d).transpose(1, 0, 3, 2, 4)

    qs, ks, gs = chunks(q, HEAD_K_B), chunks(kk, HEAD_K_B), chunks(logf, HEAD_K_B)
    vs = chunks(i, HEAD_V_B)
    tril = jnp.tril(jnp.ones((CHUNK_B, CHUNK_B), dtype=bool))

    def step(state, inp):
        qc, kc, vc, gc = inp
        b = jnp.cumsum(gc, axis=-2)
        diff = b[..., :, None, :] - b[..., None, :, :]
        decay = jnp.exp(jnp.where(tril[:, :, None], diff, -jnp.inf))
        scores = jnp.einsum('bhtsd,bhsd->bhts', qc[..., :, None, :] * decay, kc)
        o = (jnp.einsum('bhts,bhsv->bhtv', scores, vc)
             + jnp.einsum('bhtd,bhdv->bhtv', qc * jnp.exp(b), state))
        b_last = b[..., -1:, :]
        state = (jnp.exp(b_last[..., 0, :])[..., None] * state
                 + jnp.einsum('bhsd,bhsv->bhdv', kc * jnp.exp(b_last - b), vc))
        return state, o

    s0 = jnp.zeros((B, N_HEADS_B, HEAD_K_B, HEAD_V_B), jnp.float32)
    _, o = lax.scan(step, s0, (qs, ks, vs, gs))
    return o.transpose(1, 0, 3, 2, 4).reshape(B, S, N_HEADS_B, HEAD_V_B).astype(i.dtype)

def memory_attention(q, k, v):
    logits = jnp.einsum('bthd,bmhd->bhtm', q, k).astype(jnp.float32) * (HEAD_DIM_C ** -0.5)
    p = jax.nn.softmax(logits, axis=-1).astype(v.dtype)
    return jnp.einsum('bhtm,bmhd->bthd', p, v)

def hybrid_layer(x, mem, norm_in, norm_mem, w_in, q_norm_a, k_norm_a, lb,
                 o_norm_b, w_mem_kv, q_norm_c, k_norm_c, w_branch, w_out):
    B, S, _ = x.shape
    M = mem.shape[1]
    h = rms_norm(x, norm_in)
    proj = h @ w_in
    offsets = np.cumsum(IN_SPLITS)[:-1].tolist()
    (qa, ka, va, za, qi, ki, wi, qb, fb, ib, gb, qc, zc, gates) = jnp.split(proj, offsets, axis=-1)

    qa = rms_norm(qa.reshape(B, S, N_HEADS_A, HEAD_DIM_A), q_norm_a)
    ka = rms_norm(ka.reshape(B, S, N_HEADS_A, HEAD_DIM_A), k_norm_a)
    va = va.reshape(B, S, N_HEADS_A, HEAD_DIM_A)
    oa = dsa_attention(qa, ka, va, qi.reshape(B, S, N_IDX_HEADS, IDX_DIM), ki, wi)
    oa = oa.reshape(B, S, WIDTH_A) * jax.nn.silu(za)

    ob = hgrn2_recurrence(jax.nn.silu(qb), fb, ib, lb)
    ob = rms_norm(ob, o_norm_b).reshape(B, S, WIDTH_BV) * jax.nn.silu(gb)

    mkv = rms_norm(mem, norm_mem) @ w_mem_kv
    kc, vc = jnp.split(mkv, 2, axis=-1)
    kc = rms_norm(kc.reshape(B, M, N_HEADS_C, HEAD_DIM_C), k_norm_c)
    vc = vc.reshape(B, M, N_HEADS_C, HEAD_DIM_C)
    qc = rms_norm(qc.reshape(B, S, N_HEADS_C, HEAD_DIM_C), q_norm_c)
    oc = memory_attention(qc, kc, vc).reshape(B, S, WIDTH_C) * jax.nn.silu(zc)

    branches = jnp.stack([oa, ob, oc], axis=2)
    ys = jnp.einsum('bsnc,ncd->bsnd', branches, w_branch)
    g = jax.nn.sigmoid(gates.reshape(B, S, N_BRANCH, D_MODEL))
    merged = jnp.einsum('bsnd,bsnd->bsd', g, ys)
    return x + merged @ w_out

def setup_inputs(seed: int = 0) -> dict:
    key = jax.random.key(seed)
    ks = jax.random.split(key, 14)
    f32 = jnp.float32

    def gain(k, shape):
        return 1.0 + 0.1 * jax.random.normal(k, shape, f32)

    return {
        "x": jax.random.normal(ks[0], (BATCH, SEQ, D_MODEL), f32),
        "mem": jax.random.normal(ks[1], (BATCH, MEM_LEN, D_MODEL), f32),
        "norm_in": gain(ks[2], (DEPTH, D_MODEL)),
        "norm_mem": gain(ks[3], (DEPTH, D_MODEL)),
        "w_in": jax.random.normal(ks[4], (DEPTH, D_MODEL, N_IN), f32) * D_MODEL ** -0.5,
        "q_norm_a": gain(ks[5], (DEPTH, HEAD_DIM_A)),
        "k_norm_a": gain(ks[6], (DEPTH, HEAD_DIM_A)),
        "lower_bounds": 0.1 * jax.random.normal(ks[7], (DEPTH + 1, WIDTH_BK), f32),
        "o_norm_b": gain(ks[8], (DEPTH, HEAD_V_B)),
        "w_mem_kv": jax.random.normal(ks[9], (DEPTH, D_MODEL, 2 * WIDTH_C), f32) * D_MODEL ** -0.5,
        "q_norm_c": gain(ks[10], (DEPTH, HEAD_DIM_C)),
        "k_norm_c": gain(ks[11], (DEPTH, HEAD_DIM_C)),
        "w_branch": jax.random.normal(ks[12], (DEPTH, N_BRANCH, BRANCH_WIDTH, D_MODEL), f32) * BRANCH_WIDTH ** -0.5,
        "w_out": jax.random.normal(ks[13], (DEPTH, D_MODEL, D_MODEL), f32) * D_MODEL ** -0.5,
    }

def reference(x, mem, norm_in, norm_mem, w_in, q_norm_a, k_norm_a, lower_bounds,
              o_norm_b, w_mem_kv, q_norm_c, k_norm_c, w_branch, w_out):
    lb_all = jnp.cumsum(jax.nn.softmax(lower_bounds.astype(jnp.float32), axis=0), axis=0)
    for layer in range(DEPTH):
        x = hybrid_layer(x, mem, norm_in[layer], norm_mem[layer], w_in[layer],
                         q_norm_a[layer], k_norm_a[layer], lb_all[layer],
                         o_norm_b[layer], w_mem_kv[layer], q_norm_c[layer], k_norm_c[layer],
                         w_branch[layer], w_out[layer])
    return x


_drawn_inputs = setup_inputs


def setup_inputs(seed=0):
    import zlib

    import numpy as np

    out = dict(_drawn_inputs(seed))
    spreads = {}
    factors = {'norm_mem': 8.0,
     'q_norm_a': 6.148,
     'k_norm_a': 5.928,
     'lower_bounds': 46.682,
     'q_norm_c': 8.0,
     'k_norm_c': 8.0,
     'o_norm_b': 4.648}
    for name, (base, spread) in spreads.items():
        noise = np.random.default_rng([zlib.crc32(name.encode()), seed]).standard_normal(out[name].shape)
        drawn = base * np.exp(spread * noise) if base else spread * noise
        out[name] = __import__('jax').numpy.asarray(drawn.astype(out[name].dtype))
    for name, factor in factors.items():
        out[name] = (out[name] * factor).astype(out[name].dtype)
    return out
```

```python
from contextlib import ExitStack

import concourse.bass as bass
from concourse import mybir

P = 128
F32 = mybir.dt.float32
F32R = mybir.dt.float32r
BF16 = mybir.dt.bfloat16
U16 = mybir.dt.uint16
ALU = mybir.AluOpType
ACT = mybir.ActivationFunctionType
AX_X = mybir.AxisListType.X

D = 1024
S = 1024
M = 256
KT = D // P
NT = S // P
NTM = M // P
HALF = 512
WID = 512
NH = WID // P
IDX_HEADS, IDX_DIM = 8, 64
TOPK = 256
EPS = 1e-6
IDX_SCALE = IDX_DIM ** -0.5 * IDX_HEADS ** -0.5
SCALE_A = 64 ** -0.5
SCALE_C = 128 ** -0.5
BIG = 1e30
NONCAUSAL = -1e38
TAKEN = -3e38

QA, KA, VA, ZA = 0, 512, 1024, 1536
QI, KI = 2048, 2560
QB = KI + IDX_DIM + IDX_HEADS
FB, IB, GB, QC, ZC, GATES = (QB + 512 * n for n in range(1, 7))
N_KIWI = IDX_DIM + IDX_HEADS

LEVELS = [64, 32, 16, 8, 4, 2, 1]
NL = len(LEVELS)
CH = 4

IDX_TILES = list(range(TOPK // P, NT))
ROUNDS = TOPK // 8
INDEX_IN_HEAD = [[2, 3], [4, 5], [6], [7]]

ACT_LAST = {"kiwi", "qi", "kc", "vc", "qc", "fb", "ib", "gate", "ka", "va", "qa"}
SIGMOID = {"zc", "gb", "qb", "za"}


def timeline():
    t = [("job", "kiwi", 0)] + [("job", "qi", b) for b in range(4)] + [("spread",)]
    for h in range(NH):
        t += [("job", k, h) for k in ("kc", "vc", "zc", "qc")]
        t += [("index", i) for i in INDEX_IN_HEAD[h]]
        t += [("memory", h)]
    t += [("split", 0)]
    for h in range(NH):
        t += [("job", k, h) for k in ("fb", "ib", "gb", "qb")]
        for d in (2 * h, 2 * h + 1):
            t += [("job", "gate", (0, d)), ("job", "br", (0, d))]
        t += [("recur", h)]
    t += [("split", 1), ("alibi",)]
    for b in range(NH):
        t += [("job", "za", b), ("job", "ka", b), ("job", "va", b), ("keys", b), ("job", "qa", b)]
        for d in (2 * b, 2 * b + 1):
            t += [("job", "gate", (1, d)), ("job", "br", (1, d))]
        t += [("attend", b)]
    t += [("split", 2)]
    for d in range(KT):
        t += [("job", "gate", (2, d)), ("job", "br", (2, d))]
    t += [("job", "wo", (nh, kk)) for nh in range(2) for kk in range(4)]
    return t


def hybrid_layer(nc, x, mem, norm_in, norm_mem, w_in, q_norm_a, k_norm_a, lower_bounds,
                 o_norm_b, w_mem_kv, q_norm_c, k_norm_c, w_branch, w_out, merged, out):
    TL = timeline()
    JOBS = [(s[1], s[2]) for s in TL if s[0] == "job"]
    JOB = {j: n for n, j in enumerate(JOBS)}
    NJ = len(JOBS)
    WO0 = JOB[("wo", (0, 0))]
    LAST_BR = [JOB[("br", (r, KT - 1))] for r in range(3)]

    w_in_k = w_in[0].rearrange("(k p) n -> p k n", p=P)
    w_mem_k = w_mem_kv[0].rearrange("(k p) n -> p k n", p=P)
    w_br_k = w_branch[0].rearrange("b (k p) n -> b p k n", p=P)
    w_out_k = w_out[0].rearrange("(k p) n -> p k n", p=P)
    x_t = x[0].rearrange("(t p) d -> t p d", p=P)
    mem_t = mem[0].rearrange("(t p) d -> t p d", p=P)
    out_t = out[0].rearrange("(t p) d -> t p d", p=P)
    merged_t = merged.rearrange("(k p) s -> k p s", p=P)

    def weights(j):
        kind, n = JOBS[j]
        at = {"qa": QA, "ka": KA, "va": VA, "za": ZA, "qi": QI, "qb": QB, "fb": FB, "ib": IB,
              "gb": GB, "qc": QC, "zc": ZC}
        if kind in at:
            return w_in_k[:, :, at[kind] + n * P:at[kind] + (n + 1) * P]
        if kind == "kiwi":
            return w_in_k[:, :, KI:KI + N_KIWI]
        if kind == "kc":
            return w_mem_k[:, :, n * P:(n + 1) * P]
        if kind == "vc":
            return w_mem_k[:, :, WID + n * P:WID + (n + 1) * P]
        if kind == "gate":
            c = GATES + (2 - n[0]) * D + n[1] * P
            return w_in_k[:, :, c:c + P]
        if kind == "br":
            return w_br_k[2 - n[0], :, :, n[1] * P:(n[1] + 1) * P]
        return w_out_k[:, 2 * n[1]:2 * n[1] + 2, n[0] * HALF:(n[0] + 1) * HALF]

    with ExitStack() as ctx:
        sems = {}

        def sem(name):
            if name not in sems:
                sems[name] = ctx.enter_context(nc.semaphore(name))
            return sems[name]

        cur = [nc.sbuf_base]

        def sb(name, shape, dt=F32):
            n = 2 if dt == BF16 else 4
            for d in shape[1:]:
                n *= d
            cur[0] = (cur[0] + 31) // 32 * 32
            t = nc.alloc_sbuf_tensor_at(name, list(shape), dt, offset=cur[0])
            cur[0] += n
            return t

        ident = sb("ident", [P, P])
        ones_mean = sb("ones_mean", [P, P])
        ones_mean_a = sb("ones_mean_a", [P, P])
        ones_scan = sb("ones_scan", [P, P], BF16)
        pcol = sb("pcol", [P, 32])
        lbt = sb("lbt", [P, 6, 4])
        eps = sb("eps", [P, 1])
        ssq = sb("ssq", [P, NT + NTM])
        wn = sb("wn", [P, NT, IDX_HEADS])
        small = sb("small", [P, 32])
        el = sb("el", [P, NT])
        m8 = sb("m8", [P, 8])
        h_hi = sb("h_hi", [P, KT, S], F32R)
        h_lo = sb("h_lo", [P, KT, S], F32R)
        raw = sb("raw", [P, 2, D])
        w_hi = sb("w_hi", [P, 2, D], F32R)
        w_lo = sb("w_lo", [P, 2, D], F32R)

        stage1 = cur[0]
        br_hi = sb("br_hi", [P, NH, S], F32R)
        br_lo = sb("br_lo", [P, NH, S], F32R)
        g = sb("g", [P, S])
        prev = sb("prev", [P, S])
        stage1_end = cur[0]
        stage3 = cur[0]
        score_at = [P * i * (i + 1) // 2 for i in range(NT + 1)]
        score = sb("score", [P, score_at[NT]])
        o_t = sb("o_t", [P, NH, S])
        unit = cur[0]

        cur[0] = stage1
        mem_hi = sb("mem_hi", [P, KT, M], F32R)
        mem_lo = sb("mem_lo", [P, KT, M], F32R)
        qi_t = sb("qi_t", [P, 4, S])
        ki_t = sb("ki_t", [P, 2, S])
        assert cur[0] <= stage1_end
        cur[0] = unit
        relu = [sb(f"relu{i}", [P, S]) for i in range(2)]
        xt = relu
        kx, sqk, vtc = sb("kx", [P, M]), sb("sqk", [P, M]), sb("vtc", [P, M])
        vc_n = sb("vc_n", [P, NTM, P])
        qx, sqq, zc = sb("qx", [P, S]), sb("sqq", [P, S]), sb("zc", [P, S])
        pc = [sb(f"pc{i}", [P, CH, M]) for i in range(2)]
        ptc = [sb(f"ptc{i}", [P, NTM, HALF]) for i in range(2)]
        tmp, kiwi = pc[0], ptc[0]
        junk, dup, rows = pc[1], vtc, ptc[1]
        ends = [cur[0]]
        cur[0] = unit
        bq, bk, bb, bz = (sb(n, [P, S]) for n in ("bq", "bk", "bb", "bz"))
        bvn = sb("bvn", [P, NT, P])
        bvt = sb("bvt", [P, NT, P])
        bf = [sb(f"bf{i}", [P, HALF]) for i in range(2)]
        bm = [sb(f"bm{i}", [P, HALF]) for i in range(2)]
        bs, bqe, bkd, bkn = (sb(n, [P, HALF]) for n in ("bs", "bqe", "bkd", "bkn"))
        lmask = sb("lmask", [P, NL, P], BF16)
        ends.append(cur[0])
        cur[0] = unit
        q_aug, k_aug = sb("q_aug", [P, 2, S]), sb("k_aug", [P, 2, S])
        va = sb("va", [P, NT, 192])
        az = sb("az", [P, S])
        ta = [sb(f"ta{i}", [P, S]) for i in range(4)]
        rc, on = sb("rc", [P, P]), sb("on", [P, P])
        ends.append(cur[0])
        cur[0] = stage3
        m_hi, m_lo = sb("m_hi", [P, KT, S], F32R), sb("m_lo", [P, KT, S], F32R)
        xr = sb("xr", [P, 4, HALF])
        ends.append(cur[0])
        assert max(ends) <= nc.sbuf_usable_end, (ends, nc.sbuf_usable_end)

        pj = [ctx.enter_context(nc.psum_tensor(f"pj{i}", [P, S], F32)) for i in range(2)]
        px = [ctx.enter_context(nc.psum_tensor(f"px{i}", [P, S], F32)) for i in range(2)]

        g_in, g_mem = pcol[:, 0:8], pcol[:, 8:16]
        g_o, g_kc, g_ka = pcol[:, 24:25], pcol[:, 26:27], pcol[:, 28:29]
        g_qc, g_qa = pcol[:, 29:30], pcol[:, 30:31]
        lb, oml, neg_oml = lbt[:, 3, :], lbt[:, 4, :], lbt[:, 5, :]

        def freed(j):
            a = JOBS[j][0] in ACT_LAST
            n = sum((k in ACT_LAST) == a and k != "wo" for k, _ in JOBS[:j + 1])
            return (sem("slot_read_act" if a else "slot_read_dve"), n)

        def sigmoid_done(j):
            return (sem("sigmoid"), sum(k in SIGMOID for k, _ in JOBS[:j + 1]))

        def halves(n):
            return [slice(c, min(c + HALF, n)) for c in range(0, n, HALF)]

        def score_tile(i):
            return score[:, score_at[i]:score_at[i + 1]]

        def index_no(i, h):
            return IDX_TILES.index(i) * IDX_HEADS + h

        def residual_in(sp, t):
            nh, m = divmod(t, NT)
            sp.dma_start(xr[:, t % 4, :], x_t[m][:, nh * HALF:(nh + 1) * HALF]).then_inc(sem(f"res_in{t % 4}"), 16)

        def store(sp, t):
            nh, m = divmod(t, NT)
            sp.wait_ge(sem("y_sum"), t + 1)
            sp.dma_start(out_t[m][:, nh * HALF:(nh + 1) * HALF], xr[:, t % 4, :]).then_inc(sem(f"y_out{t % 4}"), 16)

        def product_no(n):
            return n // NL * (NL + 1) + 1 + n % NL

        def y_bank(m):
            return (pj + px)[m // 2][:, m % 2 * HALF:(m % 2 + 1) * HALF]

        block = ctx.enter_context(nc.Block())

        @block.sync
        def _(sp):
            def load(j):
                if j >= 2:
                    sp.wait_ge(sem("w_lo"), j - 1)
                w = weights(j)
                dst = raw[:, j % 2, 0:w.shape[1] * w.shape[2]].rearrange("p (k n) -> p k n", k=w.shape[1])
                sp.dma_start(dst, w).then_inc(sem(f"raw_in{j % 2}"), 16)

            lb2 = lower_bounds.rearrange("l (h p) -> (l h) p", p=P)
            for r0, r1, src in ((0, 8, norm_in[0].rearrange("(k p) -> k p", p=P)),
                                (8, 16, norm_mem[0].rearrange("(k p) -> k p", p=P)),
                                (16, 24, lb2), (24, 25, o_norm_b), (25, 26, q_norm_c), (26, 27, k_norm_c)):
                sp.dma_start(rows[r0:r1, 0, 0:P], src).then_inc(sem("params_in"), 16)
            for r, src in ((27, q_norm_a), (28, k_norm_a)):
                for e in range(2):
                    sp.dma_start(rows[r:r + 1, 0, 64 * e:64 * e + 64], src).then_inc(sem("params_in"), 16)
            for a in range(NT + NTM):
                if a >= 2:
                    sp.wait_ge(sem("h_turned"), a - 1)
                src = x_t[a] if a < NT else mem_t[a - NT]
                sp.dma_start(xt[a % 2][:], src).then_inc(sem(f"x_in{a % 2}"), 16)
                if a == 1:
                    load(0)
                    load(1)
            for step in TL:
                if step[0] != "job":
                    continue
                kind, n = step[1:]
                j = JOB[(kind, n)]
                if j + 2 < NJ:
                    load(j + 2)
                if kind == "gate" and n[0] > 0:
                    r, d = n
                    sp.wait_ge(sem("merged_out"), 16 * KT * r)
                    if r * KT + d > KT:
                        sp.wait_ge(sem("merged_sum"), (r - 1) * KT + d)
                    sp.dma_start(prev[:], merged_t[d]).then_inc(sem("merged_in"), 16)
                if kind == "br" and n[0] < 2:
                    r, d = n
                    if r == 0:
                        sp.wait_ge(*freed(j))
                    else:
                        sp.wait_ge(sem("merged_sum"), (r - 1) * KT + d + 1)
                    sp.dma_start(merged_t[d], g[:]).then_inc(sem("merged_out"), 16)
                if kind == "wo":
                    if n == (0, 0):
                        sp.wait_ge(sem("split_lo"), 12)
                        for t in range(4):
                            residual_in(sp, t)
                    if n[1] == 3:
                        for t in range(n[0] * NT, (n[0] + 1) * NT):
                            store(sp, t)
                            if t + 4 < 2 * NT:
                                sp.wait_ge(sem(f"y_out{t % 4}"), 16 * (t // 4 + 1))
                                residual_in(sp, t + 4)
            for s in range(4):
                sp.wait_ge(sem(f"y_out{s}"), 16 * (2 * NT // 4))
            sp.wait_ge(sem("merged_out"), 16 * KT * 2)

        @block.gpsimd
        def _(pool):
            chain = [0]

            def link(ins):
                chain[0] += 1
                ins.then_inc(sem("pool_chain"), 1)
                pool.wait_ge(sem("pool_chain"), chain[0])

            def lo(j):
                pool.wait_ge(sem("w_hi"), j + 1)
                n = weights(j).shape[1] * weights(j).shape[2]
                s = j % 2
                pool.tensor_tensor(w_lo[:, s, 0:n], raw[:, s, 0:n], w_hi[:, s, 0:n].bitcast(F32),
                                   ALU.subtract).then_inc(sem("w_lo"), 1)

            link(pool.memset(ident[:], 0.0))
            pool.affine_select(out=ident[:], in_=ident[:], compare_op=ALU.not_equal, fill=1.0, base=0,
                               pattern=[[-1, P]], channel_multiplier=1).then_inc(sem("ident"), 1)
            pool.wait_ge(sem("ident"), 1)
            link(pool.memset(eps[:], EPS))
            link(pool.memset(ones_mean[:], 1.0 / P))
            link(pool.memset(ones_scan[:], 1.0))
            link(pool.memset(ones_mean_a[:], 0.0))
            link(pool.memset(ones_mean_a[0:64, 0:64], 1.0 / 64))
            pool.memset(ones_mean_a[64:128, 64:128], 1.0 / 64).then_inc(sem("consts"), 1)
            pool.wait_ge(sem("consts"), 1)
            link(pool.tensor_copy(dup[0:64, 0:64], ident[0:64, 0:64]))
            link(pool.tensor_copy(dup[0:64, 64:128], ident[0:64, 0:64]))
            link(pool.memset(ki_t[64:128, 0, :], 0.0))
            pool.memset(ki_t[0:64, 1, :], 0.0).then_inc(sem("index_consts"), 1)
            pool.wait_ge(sem("index_consts"), 1)
            for i in range(IDX_TILES[0]):
                link(pool.memset(score_tile(i), 0.0))
                diag = score_tile(i)[:, i * P:(i + 1) * P]
                pool.affine_select(out=diag, in_=diag, compare_op=ALU.is_ge, fill=BIG, base=0,
                                   pattern=[[-1, P]], channel_multiplier=1).then_inc(sem("causal_mask"), 1)
            lo(0)
            lo(1)

            def index(i):
                pool.wait_ge(sem("index_sum"), index_no(i, IDX_HEADS - 1) + 1)
                diag = score_tile(i)[:, i * P:(i + 1) * P]
                pool.affine_select(out=diag, in_=diag, compare_op=ALU.is_ge, fill=NONCAUSAL, base=0,
                                   pattern=[[-1, P]], channel_multiplier=1).then_inc(sem("index_causal"), 1)

            def memory(h):
                for hf in range(2):
                    hh = 2 * h + hf
                    pool.wait_ge(sem("c_recip"), hh + 1)
                    r = small[:, 8 + 4 * hf:12 + 4 * hf].unsqueeze(2).broadcast_to([P, CH, M])
                    pool.tensor_tensor(pc[hf][:], pc[hf][:], r, ALU.mult).then_inc(sem("c_normed"), 1)

            def split(r):
                for h in range(NH):
                    pool.wait_ge(sem("split_hi"), r * NH + h + 1)
                    pool.tensor_tensor(br_lo[:, h, :], o_t[:, h, :], br_hi[:, h, :].bitcast(F32),
                                       ALU.subtract).then_inc(sem("split_lo"), 1)

            def level_masks():
                pool.wait_ge(sem("c_out"), 2 * NH)
                for l, m in enumerate(LEVELS):
                    nb = P // (2 * m)
                    link(pool.memset(lmask[:, l, :], 0.0))
                    v = lmask[:, l, :].rearrange("p (n two m) -> p n two m", two=2, m=m)[:, :, 1, :]
                    link(pool.memset(v, 1.0))
                    link(pool.affine_select(out=v, in_=v, compare_op=ALU.is_ge, fill=0.0, base=0,
                                            pattern=[[-2 * m, nb], [0, m]], channel_multiplier=1))
                    last = pool.affine_select(out=v, in_=v, compare_op=ALU.is_ge, fill=0.0, base=m - 1,
                                              pattern=[[2 * m, nb], [0, m]], channel_multiplier=-1)
                    last.then_inc(sem("level_masks"), 1)

            def recur(h):
                pool.wait_ge(*freed(JOB[("qb", h)]))
                pool.wait_ge(sem("b_keys"), h + 1)
                for hf in range(2):
                    hh = 2 * h + hf
                    c0 = hf * HALF
                    pool.wait_ge(sem("b_qdecay"), hh + 1)
                    pool.tensor_tensor(bqe[:], bqe[:], bq[:, c0:c0 + HALF], ALU.mult).then_inc(sem("b_qmul"), 1)
                    pool.wait_ge(sem("b_kdecay"), hh + 1)
                    pool.tensor_tensor(bkd[:], bkd[:], bk[:, c0:c0 + HALF], ALU.mult).then_inc(sem("b_kmul"), 1)
                    for l, m in enumerate(LEVELS):
                        n = hh * NL + l
                        pool.wait_ge(sem("b_exp"), n + 1)
                        if n >= 2:
                            pool.wait_ge(sem("b_product"), product_no(n - 2) + 1)
                        f = bf[n % 2][:].rearrange("p (n two m) -> p n two m", two=2, m=m)
                        o = bm[n % 2][:].rearrange("p (n two m) -> p n two m", two=2, m=m)
                        for side, src in ((0, bk), (1, bq)):
                            v = src[:, c0:c0 + HALF].rearrange("p (n two m) -> p n two m", two=2, m=m)
                            last = pool.tensor_tensor(o[:, :, side, :], f[:, :, side, :], v[:, :, side, :], ALU.mult)
                        last.then_inc(sem("b_mul"), 1)

            def alibi():
                pool.wait_ge(sem("b_out"), 2 * NH)
                pool.wait_ge(sem("split_lo"), 2 * NH)
                pool.wait_ge(sem("w_lo"), JOB[("za", 0)] + 2)
                for e in range(2):
                    slope = 2.0 ** -(e + 1)
                    for t in (q_aug, k_aug):
                        link(pool.memset(t[64:128, e, :], 0.0))
                    link(pool.memset(q_aug[64:65, e, :], -1.0))
                    link(pool.iota(q_aug[96:97, e, :], pattern=[[1, S]], base=0, channel_multiplier=0, allow_small_or_imprecise_dtypes=True))
                    link(pool.iota(k_aug[64:65, e, :], pattern=[[1, S]], base=0, channel_multiplier=0, allow_small_or_imprecise_dtypes=True))
                    link(pool.tensor_scalar(k_aug[64:65, e, :], k_aug[64:65, e, :], slope, None, ALU.mult))
                    link(pool.memset(k_aug[96:97, e, :], slope))
                pool.memset(va[:, :, 64:128], 1.0).then_inc(sem("alibi"), 1)
                pool.wait_ge(sem("alibi"), 1)

            for step in TL:
                if step[0] == "job":
                    kind, n = step[1:]
                    j = JOB[(kind, n)]
                    if j + 2 < NJ:
                        lo(j + 2)
                    if kind == "br" and n[0] == 2:
                        pool.wait_ge(sem("merged_hi"), n[1] + 1)
                        pool.tensor_tensor(m_lo[:, n[1], :], g[:], m_hi[:, n[1], :].bitcast(F32),
                                           ALU.subtract).then_inc(sem("merged_lo"), 1)
                elif step[0] == "index":
                    index(step[1])
                elif step[0] == "memory":
                    memory(step[1])
                elif step[0] == "split":
                    split(step[1])
                    if step[1] == 0:
                        level_masks()
                elif step[0] == "recur":
                    recur(step[1])
                elif step[0] == "alibi":
                    alibi()

        @block.scalar
        def _(act):
            chain = [0]

            def link(ins):
                chain[0] += 1
                ins.then_inc(sem("act_chain"), 1)
                act.wait_ge(sem("act_chain"), chain[0])

            def hi(j):
                act.wait_ge(sem(f"raw_in{j % 2}"), 16 * (j // 2 + 1))
                if j >= 2:
                    act.wait_ge(sem("proj_done"), j - 1)
                n = weights(j).shape[1] * weights(j).shape[2]
                act.activation(w_hi[:, j % 2, 0:n], raw[:, j % 2, 0:n], ACT.Copy).then_inc(sem("w_hi"), 1)

            def rsqrt(dst, src, scale=1.0):
                link(act.activation(dst, src, ACT.Ln, bias=eps[0:dst.shape[0], :], scale=scale))
                return act.activation(dst, dst, ACT.Exp, scale=-0.5)

            act.wait_ge(sem("consts"), 1)
            act.wait_ge(sem("params_turned"), 1)
            act.activation(pcol[:, 0:29], px[0][:, 0:29], ACT.Copy).then_inc(sem("params"), 1)
            act.wait_ge(sem("lb_shifted"), 1)
            act.activation(lbt[:, 1:3, :], lbt[:, 1:3, :], ACT.Exp).then_inc(sem("lb_exp"), 1)

            def rms(a):
                act.wait_ge(sem(f"x_in{a % 2}"), 16 * (a // 2 + 1))
                link(act.activation(junk[:].rearrange("p a b -> p (a b)"), xt[a % 2][:], ACT.Square,
                                    accum_out=ssq[:, a:a + 1]))
                rsqrt(ssq[:, a:a + 1], ssq[:, a:a + 1], 1.0 / D).then_inc(sem("h_rms"), 1)

            rms(0)
            rms(1)
            hi(0)
            hi(1)
            for a in range(NT + NTM):
                act.wait_ge(sem("h_gained"), a + 1)
                dst = h_hi[:, :, a * P:(a + 1) * P] if a < NT else mem_hi[:, :, (a - NT) * P:(a - NT + 1) * P]
                act.activation(dst, tmp[:].rearrange("p a (b t) -> p (a b) t", t=P), ACT.Copy).then_inc(sem("h_hi"), 1)
                if a + 2 < NT + NTM:
                    rms(a + 2)

            def spread():
                act.wait_ge(sem("index_consts"), 1)
                act.wait_ge(sem("ki_spread"), 1)
                act.activation(ki_t[0:64, 0, :], px[0][0:64, :], ACT.Copy)
                act.activation(ki_t[64:128, 1, :], px[0][64:128, :], ACT.Copy)
                v = px[1][:].rearrange("p (t c) -> p t c", c=P)[:, :, IDX_DIM:N_KIWI]
                act.activation(wn[:], v, ACT.Copy, scale=IDX_SCALE).then_inc(sem("index_in"), 1)

            def index(i):
                for h in range(IDX_HEADS):
                    q = index_no(i, h)
                    act.wait_ge(sem("index_rel"), q + 1)
                    if q >= 2:
                        act.wait_ge(sem("index_sum"), q - 1)
                    w = (i + 1) * P
                    act.activation(relu[q % 2][:, 0:w], px[q % 2][:, 0:w], ACT.Relu).then_inc(sem("index_relu"), 1)

            def memory(h):
                act.wait_ge(sem("c_kmean"), h + 1)
                act.activation(vc_n[:].rearrange("p a b -> p (a b)"), px[0][:, HALF:HALF + M], ACT.Copy)
                rsqrt(sqk[:], px[0][:, 0:M]).then_inc(sem("c_krms"), 1)
                act.wait_ge(sem("c_qmean"), h + 1)
                rsqrt(sqq[:], px[1][:]).then_inc(sem("c_qrms"), 1)
                for hf in range(2):
                    hh = 2 * h + hf
                    act.wait_ge(sem("c_max"), hh + 1)
                    for c in range(CH):
                        last = act.activation(pc[hf][:, c, :], px[hf][:, c * M:(c + 1) * M], ACT.Exp, scale=-1.0,
                                              bias=small[:, 4 * hf + c:4 * hf + c + 1],
                                              accum_out=small[:, 16 + 4 * hf + c:17 + 4 * hf + c])
                    last.then_inc(sem("c_exp"), 1)

            def split(r):
                name, per = {0: ("c_out", 2), 1: ("b_out", 2), 2: ("a_out", 16)}[r]
                if r > 0:
                    act.wait_ge(sem("proj_done"), LAST_BR[r - 1] + 1)
                for h in range(NH):
                    act.wait_ge(sem(name), per * (h + 1))
                    act.activation(br_hi[:, h, :], o_t[:, h, :], ACT.Copy).then_inc(sem("split_hi"), 1)

            def recur(h):
                act.wait_ge(sem("b_vturned"), h + 1)
                act.activation(bvn[:].rearrange("p a b -> p (a b)"), px[1][:], ACT.Copy).then_inc(sem("b_values"), 1)
                act.wait_ge(sem("b_cumsum"), h + 1)
                last = bb[:].rearrange("p (c t) -> p c t", t=P)[:, :, P - 1]
                act.activation(el[:], last, ACT.Exp).then_inc(sem("b_chunk_decay"), 1)
                for hf in range(2):
                    hh = 2 * h + hf
                    c0 = hf * HALF
                    if hh:
                        act.wait_ge(sem("b_out"), hh)
                    act.activation(bqe[:], bb[:, c0:c0 + HALF], ACT.Exp).then_inc(sem("b_qdecay"), 1)
                    act.wait_ge(sem("b_kdiff"), hh + 1)
                    act.activation(bkd[:], bkd[:], ACT.Exp).then_inc(sem("b_kdecay"), 1)
                    for l in range(NL):
                        n = hh * NL + l
                        act.wait_ge(sem("b_diff"), n + 1)
                        act.activation(bf[n % 2][:], bf[n % 2][:], ACT.Exp).then_inc(sem("b_exp"), 1)
                        if l == 2:
                            act.wait_ge(sem("b_kturned"), hh + 1)
                            act.activation(bkn[:], px[1][:, 0:HALF], ACT.Copy).then_inc(sem("b_kn"), 1)
                    act.wait_ge(sem("b_o"), hh + 1)
                    act.activation(bkd[:], px[1][:, 0:HALF], ACT.Square).then_inc(sem("b_square"), 1)
                    act.wait_ge(sem("b_mean"), hh + 1)
                    rsqrt(bkd[:], px[1][:, HALF:S]).then_inc(sem("b_rms"), 1)

            def keys(b):
                act.wait_ge(sem("a_kmean"), b + 1)
                rsqrt(ta[1][:], px[0][:]).then_inc(sem("a_krms"), 1)
                act.wait_ge(sem("alibi"), 1)
                act.wait_ge(sem("a_vturned"), b + 1)
                dst = va[:].rearrange("p t (three c) -> p t three c", three=3)[:, :, 0:3:2, :]
                act.activation(dst, px[1][:].rearrange("p (t e c) -> p t e c", t=NT, e=2), ACT.Copy).then_inc(sem("a_values"), 1)

            def attend(b):
                act.wait_ge(sem("a_qmean"), b + 1)
                rsqrt(ta[1][:], px[0][:]).then_inc(sem("a_qrms"), 1)

                def exps(u):
                    a = 16 * b + u
                    w = (u % NT + 1) * P
                    act.wait_ge(sem("a_max"), a + 1)
                    act.activation(ta[u % 2][:, 0:w], ta[u % 2][:, 0:w], ACT.Exp, scale=-1.0,
                                   bias=small[:, 24 + u % 2:25 + u % 2]).then_inc(sem("a_exp"), 1)

                exps(0)
                for u in range(16):
                    w = (u % NT + 1) * P
                    act.wait_ge(sem("a_pturned"), 16 * b + u + 1)
                    act.activation(ta[2 + u % 2][:, 0:w], px[u % 2][:, 0:w], ACT.Copy).then_inc(sem("a_pt"), 1)
                    if u + 1 < 16:
                        exps(u + 1)

            def job(kind, n):
                j = JOB[(kind, n)]
                act.wait_ge(sem("proj_done"), j + 1)
                if j + 2 < NJ:
                    hi(j + 2)
                slot = pj[j % 2]
                read = sem("slot_read_act")
                if kind == "kiwi":
                    act.activation(kiwi[0:N_KIWI].rearrange("p a b -> p (a b)"), slot[0:N_KIWI, :], ACT.Copy).then_inc(read, 1)
                elif kind == "qi":
                    act.activation(qi_t[:, n, :], slot[:], ACT.Copy).then_inc(read, 1)
                elif kind in ("kc", "vc", "qc", "zc"):
                    if n:
                        act.wait_ge(sem("c_out"), 2 * n)
                    if kind == "kc":
                        act.activation(kx[:], slot[:, 0:M], ACT.Copy)
                        act.activation(sqk[:], slot[:, 0:M], ACT.Square).then_inc(read, 1)
                    elif kind == "vc":
                        act.activation(vtc[:], slot[:, 0:M], ACT.Copy).then_inc(read, 1)
                    elif kind == "qc":
                        act.activation(qx[:], slot[:], ACT.Copy)
                        act.activation(sqq[:], slot[:], ACT.Square).then_inc(read, 1)
                    else:
                        act.activation(zc[:], slot[:], ACT.Sigmoid).then_inc(sem("sigmoid"), 1)
                elif kind in ("fb", "ib", "gb", "qb"):
                    act.wait_ge(sem("b_out") if n else sem("c_out"), 2 * n if n else 2 * NH)
                    if kind == "fb":
                        act.activation(bb[:], slot[:], ACT.Exp, scale=-1.0).then_inc(read, 1)
                    elif kind == "ib":
                        act.activation(bvt[:].rearrange("p a b -> p (a b)"), slot[:], ACT.Copy).then_inc(read, 1)
                        act.wait_ge(sem("b_keys"), n + 1)
                        act.activation(bb[:], bb[:], ACT.Ln, scale=oml[:, n:n + 1], bias=lb[:, n:n + 1]).then_inc(sem("b_logf"), 1)
                    else:
                        act.activation((bz if kind == "gb" else bq)[:], slot[:], ACT.Sigmoid).then_inc(sem("sigmoid"), 1)
                elif kind in ("ka", "va", "qa", "za"):
                    act.wait_ge(sem("a_out") if n else sem("b_out"), 16 * n if n else 2 * NH)
                    if kind == "ka":
                        act.activation(ta[0][:], slot[:], ACT.Copy)
                        act.activation(ta[1][:], slot[:], ACT.Square).then_inc(read, 1)
                    elif kind == "va":
                        act.activation(ta[2][:], slot[:], ACT.Copy).then_inc(read, 1)
                    elif kind == "qa":
                        act.wait_ge(sem("a_keys"), n + 1)
                        act.activation(ta[3][:], slot[:], ACT.Copy)
                        act.activation(ta[1][:], slot[:], ACT.Square).then_inc(read, 1)
                    else:
                        act.activation(az[:], slot[:], ACT.Sigmoid).then_inc(sem("sigmoid"), 1)
                elif kind == "gate":
                    r, d = n
                    t = r * KT + d
                    if 0 < t <= 2 * KT:
                        act.wait_ge(sem("merged_out"), 16 * t)
                    elif t:
                        act.wait_ge(sem("merged_lo"), d)
                    act.activation(g[:], slot[:], ACT.Sigmoid).then_inc(read, 1)
                elif kind == "br" and n[0] == 2:
                    act.wait_ge(sem("merged_sum"), KT + n[1] + 1)
                    if n[1] == 0:
                        act.wait_ge(sem("split_lo"), 12)
                    act.activation(m_hi[:, n[1], :], g[:], ACT.Copy).then_inc(sem("merged_hi"), 1)

            for step in TL:
                if step[0] == "job":
                    job(*step[1:])
                elif step[0] == "spread":
                    spread()
                elif step[0] == "index":
                    index(step[1])
                elif step[0] == "memory":
                    memory(step[1])
                elif step[0] == "split":
                    split(step[1])
                elif step[0] == "recur":
                    recur(step[1])
                elif step[0] == "keys":
                    keys(step[1])
                elif step[0] == "attend":
                    attend(step[1])

        @block.vector
        def _(dve):
            chain = [0]

            def link(ins):
                chain[0] += 1
                ins.then_inc(sem("dve_chain"), 1)
                dve.wait_ge(sem("dve_chain"), chain[0])

            dve.wait_ge(sem("params"), 1)
            link(dve.tensor_tensor(lbt[:, 0, :], pcol[:, 16:20], pcol[:, 20:24], ALU.max))
            dve.tensor_tensor(lbt[:, 1, :], pcol[:, 16:20], lbt[:, 0, :], ALU.subtract)
            dve.tensor_tensor(lbt[:, 2, :], pcol[:, 20:24], lbt[:, 0, :], ALU.subtract).then_inc(sem("lb_shifted"), 1)
            dve.tensor_scalar(g_qc, pcol[:, 25:26], -SCALE_C, None, ALU.mult)
            dve.tensor_scalar(g_qa, pcol[:, 27:28], -SCALE_A, None, ALU.mult)
            dve.wait_ge(sem("lb_exp"), 1)
            link(dve.tensor_tensor(lbt[:, 0, :], lbt[:, 1, :], lbt[:, 2, :], ALU.add))
            link(dve.reciprocal(lbt[:, 2, :], lbt[:, 0, :]))
            link(dve.tensor_tensor(lb, lbt[:, 1, :], lbt[:, 2, :], ALU.mult))
            link(dve.tensor_scalar(oml, lb, -1.0, 1.0, ALU.mult, ALU.add))
            link(dve.tensor_scalar(neg_oml, oml, -1.0, None, ALU.mult))

            def scale(a):
                dve.wait_ge(sem("h_rms"), a + 1)
                dve.tensor_scalar(xt[a % 2][:], xt[a % 2][:], ssq[:, a:a + 1], None, ALU.mult).then_inc(sem("h_scaled"), 1)

            scale(0)
            for a in range(NT + NTM):
                if a + 1 < NT + NTM:
                    scale(a + 1)
                gain = g_in if a < NT else g_mem
                dve.wait_ge(sem("h_turned"), a + 1)
                if a:
                    dve.wait_ge(sem("h_lo"), a)
                dve.tensor_tensor(tmp[:].rearrange("p a (b t) -> p (a b) t", t=P), px[a % 2][:].rearrange("p (k t) -> p k t", k=KT),
                                  gain.unsqueeze(2).broadcast_to([P, KT, P]), ALU.mult).then_inc(sem("h_gained"), 1)
                dve.wait_ge(sem("h_hi"), a + 1)
                if a < NT:
                    t_hi, t_lo = (t[:, :, a * P:(a + 1) * P] for t in (h_hi, h_lo))
                else:
                    t_hi, t_lo = (t[:, :, (a - NT) * P:(a - NT + 1) * P] for t in (mem_hi, mem_lo))
                dve.tensor_tensor(t_lo, tmp[:].rearrange("p a (b t) -> p (a b) t", t=P), t_hi.bitcast(F32), ALU.subtract).then_inc(sem("h_lo"), 1)

            def index(i):
                sc = score_tile(i)
                for h in range(IDX_HEADS):
                    q = index_no(i, h)
                    dve.wait_ge(sem("index_relu"), q + 1)
                    r, w = relu[q % 2][:, 0:(i + 1) * P], wn[:, i, h:h + 1]
                    if h == 0:
                        dve.tensor_scalar(sc, r, w, None, ALU.mult).then_inc(sem("index_sum"), 1)
                    else:
                        dve.wait_ge(sem("index_sum"), q)
                        dve.scalar_tensor_tensor(out=sc, in0=r, scalar=w, in1=sc, op0=ALU.mult,
                                                 op1=ALU.add).then_inc(sem("index_sum"), 1)

            done = [0]

            def topk(n, upto):
                for _ in range(n):
                    i, r = divmod(done[0], ROUNDS)
                    if i >= len(IDX_TILES) or IDX_TILES[i] > upto:
                        return
                    sc = score_tile(IDX_TILES[i])
                    if r == 0:
                        dve.wait_ge(sem("index_causal"), i + 1)
                    link(dve.max(m8[:], sc))
                    link(dve.match_replace(sc, m8[:], sc, TAKEN))
                    if r == ROUNDS - 1:
                        link(dve.tensor_scalar(sc, sc, 0.99 * TAKEN, BIG, ALU.is_gt, ALU.mult))
                    done[0] += 1

            def memory(h):
                dve.wait_ge(sem("c_krms"), h + 1)
                dve.scalar_tensor_tensor(out=kx[:], in0=kx[:], scalar=g_kc, in1=sqk[:], op0=ALU.mult, op1=ALU.mult)
                dve.wait_ge(sem("c_qrms"), h + 1)
                dve.scalar_tensor_tensor(out=qx[:], in0=qx[:], scalar=g_qc, in1=sqq[:], op0=ALU.mult,
                                         op1=ALU.mult).then_inc(sem("c_qk"), 1)
                for hf in range(2):
                    hh = 2 * h + hf
                    dve.wait_ge(sem("c_logits"), hh + 1)
                    dve.tensor_reduce(small[:, 4 * hf:4 * hf + 4], px[hf][:].rearrange("p (c m) -> p c m", m=M),
                                      AX_X, ALU.min).then_inc(sem("c_max"), 1)
                for hf in range(2):
                    hh = 2 * h + hf
                    dve.wait_ge(sem("c_exp"), hh + 1)
                    dve.reciprocal(small[:, 8 + 4 * hf:12 + 4 * hf], small[:, 16 + 4 * hf:20 + 4 * hf]).then_inc(sem("c_recip"), 1)
                for hf in range(2):
                    hh = 2 * h + hf
                    dve.wait_ge(sem("c_pturned"), hh + 1)
                    dve.tensor_copy(ptc[hf][:].rearrange("p a b -> p (a b)"), px[hf][:]).then_inc(sem("c_pt"), 1)
                for hf in range(2):
                    hh = 2 * h + hf
                    c0 = hf * HALF
                    dve.wait_ge(sem("c_o"), hh + 1)
                    dve.tensor_tensor(o_t[:, h, c0:c0 + HALF], px[hf][:, 0:HALF], zc[:, c0:c0 + HALF],
                                      ALU.mult).then_inc(sem("c_out"), 1)

            def recur(h):
                def diffs(hh, l):
                    n = hh * NL + l
                    m = LEVELS[l]
                    c0 = hh % 2 * HALF
                    if n >= 2:
                        dve.wait_ge(sem("b_mul"), n - 1)
                    v = bb[:, c0:c0 + HALF].rearrange("p (n two m) -> p n two m", two=2, m=m)
                    f = bf[n % 2][:].rearrange("p (n two m) -> p n two m", two=2, m=m)
                    mid = v[:, :, 0, m - 1:m].broadcast_to([P, HALF // (2 * m), m])
                    dve.tensor_tensor(f[:, :, 0, :], mid, v[:, :, 0, :], ALU.subtract)
                    dve.tensor_tensor(f[:, :, 1, :], v[:, :, 1, :], mid, ALU.subtract).then_inc(sem("b_diff"), 1)

                def gather(hh, l):
                    p = hh * (NL + 1) + 1 + l
                    dve.wait_ge(sem("b_product"), p + 1)
                    src = px[0][:, p % 2 * HALF:(p % 2 + 1) * HALF].rearrange("p (c t) -> p c t", t=P)
                    dst = bs[:].rearrange("p (c t) -> p c t", t=P)
                    if l < 0:
                        dve.tensor_tensor(dst, src, ident[:].unsqueeze(1).broadcast_to([P, CH, P]),
                                          ALU.mult).then_inc(sem("b_gather"), 1)
                    else:
                        dve.wait_ge(sem("b_gather"), p)
                        mask = lmask[:, l, :].bitcast(U16).unsqueeze(1).broadcast_to([P, CH, P])
                        dve.copy_predicated(dst, mask, src).then_inc(sem("b_gather"), 1)

                for hf in range(2):
                    hh = 2 * h + hf
                    c0 = hf * HALF
                    v = bb[:, c0:c0 + HALF].rearrange("p (c t) -> p c t", t=P)
                    if hh:
                        dve.wait_ge(sem("b_out"), hh)
                    dve.tensor_tensor(bkd[:].rearrange("p (c t) -> p c t", t=P),
                                      v[:, :, P - 1:P].broadcast_to([P, CH, P]), v, ALU.subtract).then_inc(sem("b_kdiff"), 1)
                    diffs(hh, 0)
                    diffs(hh, 1)
                    if h == 0 and hf == 0:
                        dve.wait_ge(sem("level_masks"), NL)
                    gather(hh, -1)
                    for l in range(NL):
                        if l + 2 < NL:
                            diffs(hh, l + 2)
                        gather(hh, l)
                        if l == 3:
                            dve.wait_ge(sem("b_kv"), hh + 1)
                            dve.wait_ge(sem("b_chunk_decay"), h + 1)
                            for c in range(CH * hf, min(CH * hf + CH, NT - 1)):
                                kv = px[1][:, HALF + c % CH * P:HALF + (c % CH + 1) * P]
                                if c == 0:
                                    dve.tensor_copy(bvt[:, 1, :], kv).then_inc(sem("b_state"), 1)
                                else:
                                    dve.wait_ge(sem("b_state"), h * (NT - 1) + c)
                                    dve.scalar_tensor_tensor(out=bvt[:, c + 1, :], in0=bvt[:, c, :], scalar=el[:, c:c + 1],
                                                             in1=kv, op0=ALU.mult, op1=ALU.add).then_inc(sem("b_state"), 1)
                    topk(2, NT)
                    dve.wait_ge(sem("b_rms"), hh + 1)
                    link(dve.scalar_tensor_tensor(out=bqe[:], in0=px[1][:, 0:HALF], scalar=g_o, in1=bkd[:],
                                                  op0=ALU.mult, op1=ALU.mult))
                    if hh == 0:
                        dve.wait_ge(sem("split_lo"), NH)
                    dve.tensor_tensor(o_t[:, h, c0:c0 + HALF], bqe[:], bz[:, c0:c0 + HALF], ALU.mult).then_inc(sem("b_out"), 1)

            def normed_heads(dst, src, gain, rms):
                for e in range(2):
                    p = slice(64 * e, 64 * e + 64)
                    last = dve.scalar_tensor_tensor(out=dst[0:64, e, :], in0=src[p, :], scalar=gain[p, :], in1=rms[p, :],
                                                    op0=ALU.mult, op1=ALU.mult)
                return last

            def keys(b):
                dve.wait_ge(sem("alibi"), 1)
                if b:
                    link(dve.tensor_scalar(k_aug[64:128, :, :], k_aug[64:128, :, :], 0.25, None, ALU.mult))
                dve.wait_ge(sem("a_krms"), b + 1)
                normed_heads(k_aug, ta[0], g_ka, ta[1]).then_inc(sem("a_keys"), 1)

            def attend(b):
                dve.wait_ge(sem("a_qrms"), b + 1)
                normed_heads(q_aug, ta[3], g_qa, ta[1]).then_inc(sem("a_queries"), 1)

                def mask(u):
                    a, i = 16 * b + u, u % NT
                    w = (i + 1) * P
                    if b == 0 and i < IDX_TILES[0]:
                        dve.wait_ge(sem("causal_mask"), i + 1)
                    dve.wait_ge(sem("a_logits"), a + 1)
                    dve.tensor_tensor_reduce(ta[u % 2][:, 0:w], px[u % 2][:, 0:w], score_tile(i), 1.0, 3e38, ALU.add,
                                             ALU.min, small[:, 24 + u % 2:25 + u % 2]).then_inc(sem("a_max"), 1)

                mask(0)
                for u in range(16):
                    if u + 1 < 16:
                        mask(u + 1)
                    e, i = divmod(u, NT)
                    own, other = slice(64 * e, 64 * e + 64), slice(64 - 64 * e, 128 - 64 * e)
                    dve.wait_ge(sem("a_o"), 16 * b + u + 1)
                    link(dve.reciprocal(rc[own, :], px[u % 2][other, 0:P]))
                    link(dve.tensor_tensor(on[own, :], px[u % 2][own, 0:P], rc[own, :], ALU.mult))
                    if b == 0 and u == 0:
                        dve.wait_ge(sem("split_lo"), 2 * NH)
                    dve.tensor_tensor(o_t[own, b, i * P:(i + 1) * P], on[own, :], az[own, i * P:(i + 1) * P],
                                      ALU.mult).then_inc(sem("a_out"), 1)

            def job(kind, n):
                j = JOB[(kind, n)]
                slot = pj[j % 2]
                if kind in SIGMOID:
                    buf = {"zc": zc, "gb": bz, "qb": bq, "za": az}[kind]
                    dve.wait_ge(*sigmoid_done(j))
                    dve.tensor_tensor(buf[:], buf[:], slot[:], ALU.mult).then_inc(sem("slot_read_dve"), 1)
                elif kind == "fb":
                    dve.wait_ge(*freed(j))
                    link(dve.tensor_scalar(bb[:], bb[:], 1.0, None, ALU.add))
                    link(dve.reciprocal(bb[:], bb[:]))
                    dve.tensor_scalar(bk[:], bb[:], neg_oml[:, n:n + 1], oml[:, n:n + 1], ALU.mult,
                                      ALU.add).then_inc(sem("b_keys"), 1)
                elif kind == "ib":
                    dve.wait_ge(sem("b_logf"), n + 1)
                    for c in range(NT):
                        v = bb[:, c * P:(c + 1) * P]
                        last = dve.tensor_tensor_scan(v, ones_scan[:], v, 0.0, ALU.mult, ALU.add)
                    last.then_inc(sem("b_cumsum"), 1)
                elif kind == "br":
                    r, d = n
                    dve.wait_ge(sem("proj_done"), j + 1)
                    dve.wait_ge(*freed(j - 1))
                    dve.tensor_tensor(g[:], g[:], slot[:], ALU.mult).then_inc(sem("slot_read_dve"), 1)
                    if r:
                        dve.wait_ge(*freed(j))
                        dve.wait_ge(sem("merged_in"), 16 * ((r - 1) * KT + d + 1))
                        dve.tensor_tensor(g[:], g[:], prev[:], ALU.add).then_inc(sem("merged_sum"), 1)
                if kind in ("kc", "vc", "zc", "qc"):
                    topk(3, INDEX_IN_HEAD[n][0] - 1)
                elif kind in ("fb", "ib", "gb", "qb", "gate", "br") and (kind not in ("gate", "br") or n[0] == 0):
                    topk(5, NT)

            for step in TL:
                if step[0] == "job":
                    if step[1] == "wo":
                        break
                    job(*step[1:])
                elif step[0] == "index":
                    index(step[1])
                elif step[0] == "memory":
                    memory(step[1])
                elif step[0] == "recur":
                    recur(step[1])
                elif step[0] == "alibi":
                    topk(len(IDX_TILES) * ROUNDS, NT)
                elif step[0] == "keys":
                    keys(step[1])
                elif step[0] == "attend":
                    attend(step[1])
            for t in range(2 * NT):
                nh, m = divmod(t, NT)
                if m < NT - 1:
                    dve.wait_ge(sem("y_proj"), nh * (NT - 1) + m + 1)
                else:
                    dve.wait_ge(sem("proj_done"), WO0 + 4 * (nh + 1))
                dve.wait_ge(sem(f"res_in{t % 4}"), 16 * (t // 4 + 1))
                dve.tensor_tensor(xr[:, t % 4, :], xr[:, t % 4, :], y_bank(t % NT), ALU.add).then_inc(sem("y_sum"), 1)

        @block.tensor
        def _(pe):
            def three(out, a_hi, a_lo, b_hi, b_lo, first, last):
                pe.matmul(out, a_hi, b_hi, start=first, stop=False)
                pe.matmul(out, a_hi, b_lo, start=False, stop=False)
                return pe.matmul(out, a_lo, b_hi, start=False, stop=last)

            pe.wait_ge(sem("ident"), 1)
            pe.wait_ge(sem("params_in"), 16 * 10)
            pe.transpose(px[0][:, 0:29], rows[0:29, 0, 0:P], ident[0:29, 0:29]).then_inc(sem("params_turned"), 1)
            for a in range(NT + NTM):
                pe.wait_ge(sem("h_scaled"), a + 1)
                if a == 0:
                    pe.wait_ge(sem("params"), 1)
                if a >= 2:
                    pe.wait_ge(sem("h_gained"), a - 1)
                for k in range(KT):
                    last = pe.transpose(px[a % 2][:, k * P:(k + 1) * P], xt[a % 2][:, k * P:(k + 1) * P], ident[:])
                last.then_inc(sem("h_turned"), 1)

            def job(kind, n):
                j = JOB[(kind, n)]
                s = j % 2
                pe.wait_ge(sem("w_lo"), j + 1)
                if j >= 2 and j < WO0:
                    pe.wait_ge(*freed(j - 2))
                if kind == "wo":
                    return output(*n)
                hi, lo, cols = h_hi, h_lo, S
                if kind in ("kc", "vc"):
                    hi, lo, cols = mem_hi, mem_lo, M
                if kind == "br":
                    hi, lo = br_hi, br_lo
                    pe.wait_ge(sem("split_lo"), NH * (n[0] + 1))
                if j == 0:
                    pe.wait_ge(sem("h_lo"), NT)
                if kind == "kc" and n == 0:
                    pe.wait_ge(sem("h_lo"), NT + NTM)
                kt, m = weights(j).shape[1:]
                for c in halves(cols):
                    for k in range(kt):
                        last = three(pj[s][0:m, c], w_hi[:, s, k * m:(k + 1) * m], w_lo[:, s, k * m:(k + 1) * m],
                                     hi[:, k, c], lo[:, k, c], k == 0, k == kt - 1)
                last.then_inc(sem("proj_done"), 1)

            def output(nh, kk):
                s = (WO0 + nh * 4 + kk) % 2
                if nh == 0 and kk == 0:
                    pe.wait_ge(*freed(WO0 - 1))
                    pe.wait_ge(*freed(WO0 - 2))
                    pe.wait_ge(sem("merged_lo"), KT)
                for m in range(NT):
                    if nh and kk == 0:
                        pe.wait_ge(sem("y_sum"), m + 1)
                    t = slice(m * P, (m + 1) * P)
                    for k2 in range(2):
                        k = 2 * kk + k2
                        c = slice(k2 * HALF, (k2 + 1) * HALF)
                        last = three(y_bank(m), m_hi[:, k, t], m_lo[:, k, t], w_hi[:, s, c], w_lo[:, s, c],
                                     k == 0, k == KT - 1)
                    if kk == 3 and m < NT - 1:
                        last.then_inc(sem("y_proj"), 1)
                last.then_inc(sem("proj_done"), 1)

            def spread():
                pe.wait_ge(*freed(JOB[("kiwi", 0)]))
                pe.wait_ge(sem("index_consts"), 1)
                pe.wait_ge(sem("h_gained"), NT + NTM)
                for c in range(2):
                    pe.matmul(px[0][:, c * HALF:(c + 1) * HALF], dup[0:64, 0:P], kiwi[0:64, c, :], start=True, stop=True)
                kf = kiwi[:].rearrange("p a b -> p (a b)")
                for i in range(NT):
                    last = pe.transpose(px[1][:, i * P:i * P + N_KIWI], kf[0:N_KIWI, i * P:(i + 1) * P],
                                        ident[0:N_KIWI, 0:N_KIWI])
                last.then_inc(sem("ki_spread"), 1)

            def index(i, h_c):
                if h_c:
                    pe.wait_ge(sem("c_out"), 2 * h_c)
                else:
                    pe.wait_ge(sem("index_in"), 1)
                pe.wait_ge(*freed(JOB[("qi", 3)]))
                for h in range(IDX_HEADS):
                    q = index_no(i, h)
                    if q >= 2:
                        pe.wait_ge(sem("index_relu"), q - 1)
                    for c in halves((i + 1) * P):
                        last = pe.matmul(px[q % 2][:, c], qi_t[:, h // 2, i * P:(i + 1) * P], ki_t[:, h % 2, c],
                                         start=True, stop=True)
                    last.then_inc(sem("index_rel"), 1)

            def memory(h, n_index):
                pe.wait_ge(*freed(JOB[("vc", h)]))
                pe.wait_ge(sem("index_relu"), n_index)
                pe.wait_ge(sem("consts"), 1)
                pe.matmul(px[0][:, 0:M], ones_mean[:], sqk[:], start=True, stop=True)
                for t in range(NTM):
                    last = pe.transpose(px[0][:, HALF + t * P:HALF + (t + 1) * P], vtc[:, t * P:(t + 1) * P], ident[:])
                last.then_inc(sem("c_kmean"), 1)
                pe.wait_ge(*freed(JOB[("qc", h)]))
                for c in halves(S):
                    last = pe.matmul(px[1][:, c], ones_mean[:], sqq[:, c], start=True, stop=True)
                last.then_inc(sem("c_qmean"), 1)
                pe.wait_ge(sem("c_qk"), h + 1)
                for hf in range(2):
                    for c in range(CH):
                        t = (hf * CH + c) * P
                        last = pe.matmul(px[hf][:, c * M:(c + 1) * M], qx[:, t:t + P], kx[:], start=True, stop=True)
                    last.then_inc(sem("c_logits"), 1)
                for hf in range(2):
                    pe.wait_ge(sem("c_normed"), 2 * h + hf + 1)
                    for mb in range(NTM):
                        for c in range(CH):
                            last = pe.transpose(px[hf][:, mb * HALF + c * P:mb * HALF + (c + 1) * P],
                                                pc[hf][:, c, mb * P:(mb + 1) * P], ident[:])
                    last.then_inc(sem("c_pturned"), 1)
                for hf in range(2):
                    pe.wait_ge(sem("c_pt"), 2 * h + hf + 1)
                    for mb in range(NTM):
                        last = pe.matmul(px[hf][:, 0:HALF], vc_n[:, mb, :], ptc[hf][:, mb, :], start=mb == 0, stop=mb == NTM - 1)
                    last.then_inc(sem("c_o"), 1)

            def recur(h):
                def products(hh, l):
                    p = hh * (NL + 1) + 1 + l
                    c0 = hh % 2 * HALF
                    if p >= 2:
                        pe.wait_ge(sem("b_gather"), p - 1)
                    if l >= 0:
                        pe.wait_ge(sem("b_mul"), hh * NL + l + 1)
                    for c in range(CH):
                        o = px[0][:, p % 2 * HALF + c * P:p % 2 * HALF + (c + 1) * P]
                        if l < 0:
                            k, q = (t[:, c0 + c * P:c0 + (c + 1) * P] for t in (bk, bq))
                        else:
                            k = q = bm[(hh * NL + l) % 2][:, c * P:(c + 1) * P]
                        last = pe.matmul(o, k, q, start=True, stop=True)
                    last.then_inc(sem("b_product"), 1)

                pe.wait_ge(*freed(JOB[("ib", h)]))
                pe.wait_ge(sem("b_out") if h else sem("c_out"), 2 * h if h else 2 * NH)
                for c in range(NT):
                    last = pe.transpose(px[1][:, c * P:(c + 1) * P], bvt[:, c, :], ident[:])
                last.then_inc(sem("b_vturned"), 1)
                pe.wait_ge(*freed(JOB[("qb", h)]))
                pe.wait_ge(sem("b_keys"), h + 1)
                for hf in range(2):
                    hh = 2 * h + hf
                    products(hh, -1)
                    products(hh, 0)
                    pe.wait_ge(sem("b_kmul"), hh + 1)
                    pe.wait_ge(sem("b_values"), h + 1)
                    if hh:
                        pe.wait_ge(sem("b_out"), hh)
                    for c in range(CH):
                        last = pe.transpose(px[1][:, c * P:(c + 1) * P], bkd[:, c * P:(c + 1) * P], ident[:])
                    last.then_inc(sem("b_kturned"), 1)
                    products(hh, 1)
                    products(hh, 2)
                    pe.wait_ge(sem("b_kn"), hh + 1)
                    for c in range(CH):
                        last = pe.matmul(px[1][:, HALF + c * P:HALF + (c + 1) * P], bkn[:, c * P:(c + 1) * P],
                                         bvn[:, hf * CH + c, :], start=True, stop=True)
                    last.then_inc(sem("b_kv"), 1)
                    for l in range(3, NL):
                        products(hh, l)
                    pe.wait_ge(sem("b_gather"), (hh + 1) * (NL + 1))
                    pe.wait_ge(sem("b_qmul"), hh + 1)
                    for c in range(CH):
                        n = hf * CH + c
                        o = px[1][:, c * P:(c + 1) * P]
                        last = pe.matmul(o, bvn[:, n, :], bs[:, c * P:(c + 1) * P], start=True, stop=n == 0)
                        if n:
                            pe.wait_ge(sem("b_state"), h * (NT - 1) + n)
                            last = pe.matmul(o, bvt[:, n, :], bqe[:, c * P:(c + 1) * P], start=False, stop=True)
                    last.then_inc(sem("b_o"), 1)
                    pe.wait_ge(sem("b_square"), hh + 1)
                    pe.wait_ge(sem("b_state"), h * (NT - 1) + min(CH * hf + CH, NT - 1))
                    pe.matmul(px[1][:, HALF:S], ones_mean[:], bkd[:], start=True, stop=True).then_inc(sem("b_mean"), 1)

            def keys(b):
                pe.wait_ge(*freed(JOB[("ka", b)]))
                pe.wait_ge(sem("a_out") if b else sem("b_out"), 16 * b if b else 2 * NH)
                for c in halves(S):
                    last = pe.matmul(px[0][:, c], ones_mean_a[:], ta[1][:, c], start=True, stop=True)
                last.then_inc(sem("a_kmean"), 1)
                pe.wait_ge(*freed(JOB[("va", b)]))
                for i in range(NT):
                    last = pe.transpose(px[1][:, i * P:(i + 1) * P], ta[2][:, i * P:(i + 1) * P], ident[:])
                last.then_inc(sem("a_vturned"), 1)

            def attend(b):
                pe.wait_ge(*freed(JOB[("qa", b)]))
                pe.wait_ge(sem("a_krms"), b + 1)
                for c in halves(S):
                    last = pe.matmul(px[0][:, c], ones_mean_a[:], ta[1][:, c], start=True, stop=True)
                last.then_inc(sem("a_qmean"), 1)
                pe.wait_ge(sem("a_queries"), b + 1)
                pe.wait_ge(sem("a_values"), b + 1)

                def logits(u):
                    e, i = divmod(u, NT)
                    if u >= 2:
                        pe.wait_ge(sem("a_out"), 16 * b + u - 1)
                    for c in halves((i + 1) * P):
                        last = pe.matmul(px[u % 2][:, c], q_aug[:, e, i * P:(i + 1) * P], k_aug[:, e, c],
                                         start=True, stop=True)
                    last.then_inc(sem("a_logits"), 1)

                logits(0)
                for u in range(16):
                    a = 16 * b + u
                    e, i = divmod(u, NT)
                    pe.wait_ge(sem("a_exp"), a + 1)
                    for k in range(i + 1):
                        last = pe.transpose(px[u % 2][:, k * P:(k + 1) * P], ta[u % 2][:, k * P:(k + 1) * P], ident[:])
                    last.then_inc(sem("a_pturned"), 1)
                    if u + 1 < 16:
                        logits(u + 1)
                    pe.wait_ge(sem("a_pt"), a + 1)
                    for k in range(i + 1):
                        last = pe.matmul(px[u % 2][:, 0:P], va[:, k, 64 * e:64 * e + P], ta[2 + u % 2][:, k * P:(k + 1) * P],
                                         start=k == 0, stop=k == i)
                    last.then_inc(sem("a_o"), 1)

            n_index = h_c = 0
            for step in TL:
                if step[0] == "job":
                    job(*step[1:])
                elif step[0] == "spread":
                    spread()
                elif step[0] == "index":
                    index(step[1], h_c)
                    n_index += IDX_HEADS
                elif step[0] == "memory":
                    memory(step[1], n_index)
                    h_c += 1
                elif step[0] == "recur":
                    recur(step[1])
                elif step[0] == "keys":
                    keys(step[1])
                elif step[0] == "attend":
                    attend(step[1])


_INS = ["x", "mem", "norm_in", "norm_mem", "w_in", "q_norm_a", "k_norm_a", "lower_bounds", "o_norm_b",
        "w_mem_kv", "q_norm_c", "k_norm_c", "w_branch", "w_out"]


def kernel(**inputs):
    import numpy as _np
    import concourse.bacc as _bacc
    from concourse.bass_utils import run_bass_kernel_spmd as _run

    nc = _bacc.Bacc("TRN2", target_bir_lowering=False, num_devices=1)
    arrays, args = {}, []
    for name in _INS:
        a = _np.ascontiguousarray(inputs[name])
        arrays[f"in_{name}"] = a
        args.append(nc.dram_tensor(f"in_{name}", a.shape, mybir.dt.from_np(a.dtype), kind="ExternalInput").ap())
    args.append(nc.dram_tensor("merged", [D, S], F32, kind="Internal").ap())
    args.append(nc.dram_tensor("out_0", [1, S, D], F32, kind="ExternalOutput").ap())
    hybrid_layer(nc, *args)
    r = _run(nc, [arrays], core_ids=[0])
    return r.results[0]["out_0"]
```

```python
from contextlib import ExitStack

import concourse.bass as bass
from concourse import mybir

P = 128
F32 = mybir.dt.float32
F32R = mybir.dt.float32r
BF16 = mybir.dt.bfloat16
U16 = mybir.dt.uint16
ALU = mybir.AluOpType
ACT = mybir.ActivationFunctionType
AX_X = mybir.AxisListType.X

D = 1024
S = 1024
M = 256
KT = D // P
NT = S // P
NTM = M // P
HALF = 512
WID = 512
NH = WID // P
IDX_HEADS, IDX_DIM = 8, 64
TOPK = 256
EPS = 1e-6
IDX_SCALE = IDX_DIM ** -0.5 * IDX_HEADS ** -0.5
SCALE_A = 64 ** -0.5
SCALE_C = 128 ** -0.5
BIG = 1e30
NONCAUSAL = -1e38
TAKEN = -3e38

QA, KA, VA, ZA = 0, 512, 1024, 1536
QI, KI = 2048, 2560
QB = KI + IDX_DIM + IDX_HEADS
FB, IB, GB, QC, ZC, GATES = (QB + 512 * n for n in range(1, 7))
N_KIWI = IDX_DIM + IDX_HEADS

LEVELS = [64, 32, 16, 8, 4, 2, 1]
NL = len(LEVELS)
CH = 4

IDX_TILES = list(range(TOPK // P, NT))
ROUNDS = TOPK // 8


ACT_LAST = {"kiwi", "qi", "kc", "vc", "qc", "fb", "ib", "gate", "ka", "va", "qa", "index"}
GATED = {"zc", "gb", "qb", "za"}

REC_LEVELS = [[0], [1, 2], [3], [4], [5, 6], [], []]
REC_PARTS = len(REC_LEVELS)
INDEX_FIRST = 16
FB_PART = 12
REC_JOBS = (3, 5, 8, 9)
ATT_JOBS = (1, 6, 9, 13)
FILL = {'key': 2, 'qmean': 5, 'rows': 3, 'level': 4, 'keys': 4, 'output': 2, 'square': 2, 'mean': 8, 'query': 10, 'probs': 2, 'turned': 1}
TOPK_JOB = {'kc': (20, 26), 'vc': (20, 20), 'qc': (36, 32), 'zc': (6, 6), 'fb': (20, 18), 'ib': (25, 10), 'gb': (20, 10), 'qb': (15, 10), 'ka': (25, 0), 'va': (25, 0), 'qa': (25, 0)}
TOPK_LEVEL = (4, 4, 4, 1, 3)
TOPK_REC = (0, 2, 2, 2, 0, 5, 5)
TOPK_MEMORY = (4, 4, 5, 8)
TOPK_DECAY = 35
TOPK_ATT = 10
ROWS_AHEAD = 4


def timeline():
    t = [("rows", a) for a in range(NT)] + [("job", "kiwi", 0), ("job", "qi", 0)]
    t += [("rows", NT + a) for a in range(NTM)]
    t += [("job", "qi", b) for b in range(1, 4)] + [("spread",)]
    index = [("index", i, h) for i in IDX_TILES for h in range(IDX_HEADS)]
    t += index[:INDEX_FIRST]
    index = index[INDEX_FIRST:]
    per = len(index) // NH
    for h in range(NH):
        t += [("job", k, h) for k in ("kc", "vc", "qc", "zc")]
        mine = index[h * per:(h + 1) * per]
        for part in range(4):
            t += [("memory", h, part)] + mine[part * per // 4:(part + 1) * per // 4]
    for h in range(NH):
        for n, k in enumerate(("fb", "ib", "gb", "qb")):
            if k != "fb" or h == 0:
                t += [("job", k, h)]
            if h == 0:
                t += [("split", 0, n)]
        fill = [("job", k, (0, d)) for d in (2 * h, 2 * h + 1) for k in ("gate", "br")]
        for part in range(2 * REC_PARTS):
            t += [("recur", h, part)]
            if part in REC_JOBS:
                t += [fill.pop(0)]
            if part == FB_PART and h + 1 < NH:
                t += [("job", "fb", h + 1)]
    for b in range(NH):
        steps = [("job", "za", b), ("job", "ka", b), ("job", "va", b), ("keys", b), ("job", "qa", b), ("queries", b)]
        if b == 0:
            steps[1:1] = [("alibi",), ("split", 1, 0)]
            steps[4:4] = [("split", 1, 1)]
            steps[6:6] = [("positions",)]
            steps[9:9] = [("split", 1, 2), ("split", 1, 3)]
        t += steps
        fill = [("job", k, (1, d)) for d in (2 * b, 2 * b + 1) for k in ("gate", "br")]
        for u in range(2 * NT):
            t += [("attend", b, u)]
            if u in ATT_JOBS:
                t += [fill.pop(0)]
    at = len(t) - 1
    t[at:at] = [("split", 2, h) for h in range(NH - 1)]
    t += [("split", 2, NH - 1)]
    for d in range(KT):
        t += [("job", "gate", (2, d)), ("job", "br", (2, d))]
    t += [("job", "wo", (nh, kk)) for nh in range(2) for kk in range(4)]
    return t


def hybrid_layer(nc, x, mem, norm_in, norm_mem, w_in, q_norm_a, k_norm_a, lower_bounds,
                 o_norm_b, w_mem_kv, q_norm_c, k_norm_c, w_branch, w_out, merged, out):
    TL = timeline()
    JOBS = [(s[1], s[2]) for s in TL if s[0] == "job"]
    JOB = {j: n for n, j in enumerate(JOBS)}
    NJ = len(JOBS)
    USES = [(s[1], s[2]) if s[0] == "job" else s for s in TL if s[0] in ("job", "index")]
    SLOT = {u: n for n, u in enumerate(USES)}
    WO0 = JOB[("wo", (0, 0))]
    LAST_BR = [JOB[("br", (r, KT - 1))] for r in range(3)]

    w_in_k = w_in[0].rearrange("(k p) n -> p k n", p=P)
    w_mem_k = w_mem_kv[0].rearrange("(k p) n -> p k n", p=P)
    w_br_k = w_branch[0].rearrange("b (k p) n -> b p k n", p=P)
    w_out_k = w_out[0].rearrange("(k p) n -> p k n", p=P)
    x_t = x[0].rearrange("(t p) d -> t p d", p=P)
    mem_t = mem[0].rearrange("(t p) d -> t p d", p=P)
    out_t = out[0].rearrange("(t p) d -> t p d", p=P)
    merged_t = merged.rearrange("(k p) s -> k p s", p=P)

    def weights(j):
        kind, n = JOBS[j]
        at = {"qa": QA, "ka": KA, "va": VA, "za": ZA, "qi": QI, "qb": QB, "fb": FB, "ib": IB,
              "gb": GB, "qc": QC, "zc": ZC}
        if kind in at:
            return w_in_k[:, :, at[kind] + n * P:at[kind] + (n + 1) * P]
        if kind == "kiwi":
            return w_in_k[:, :, KI:KI + N_KIWI]
        if kind == "kc":
            return w_mem_k[:, :, n * P:(n + 1) * P]
        if kind == "vc":
            return w_mem_k[:, :, WID + n * P:WID + (n + 1) * P]
        if kind == "gate":
            c = GATES + (2 - n[0]) * D + n[1] * P
            return w_in_k[:, :, c:c + P]
        if kind == "br":
            return w_br_k[2 - n[0], :, :, n[1] * P:(n[1] + 1) * P]
        return w_out_k[:, 2 * n[1]:2 * n[1] + 2, n[0] * HALF:(n[0] + 1) * HALF]

    with ExitStack() as ctx:
        sems = {}

        def sem(name):
            if name not in sems:
                sems[name] = ctx.enter_context(nc.semaphore(name))
            return sems[name]

        cur = [nc.sbuf_base]

        def sb(name, shape, dt=F32):
            n = 2 if dt == BF16 else 4
            for d in shape[1:]:
                n *= d
            cur[0] = (cur[0] + 31) // 32 * 32
            t = nc.alloc_sbuf_tensor_at(name, list(shape), dt, offset=cur[0])
            cur[0] += n
            return t

        ident = sb("ident", [P, P])
        ones_mean = sb("ones_mean", [P, P])
        ones_mean_a = sb("ones_mean_a", [P, P])
        ones_scan = sb("ones_scan", [P, P], BF16)
        pcol = sb("pcol", [P, 32])
        lbt = sb("lbt", [P, 6, 4])
        eps = sb("eps", [P, 1])
        ssq = sb("ssq", [P, NT + NTM])
        wn = sb("wn", [P, NT, IDX_HEADS])
        small = sb("small", [P, 32])
        el = sb("el", [P, NT])
        m8 = sb("m8", [P, 8])
        h_hi = sb("h_hi", [P, KT, S], F32R)
        h_lo_at = cur[0]
        h_lo = sb("h_lo", [P, KT, S], F32R)
        raw = sb("raw", [P, 2, D])
        w_hi = sb("w_hi", [P, 2, D], F32R)
        w_lo = sb("w_lo", [P, 2, D], F32R)

        stage1 = cur[0]
        br_hi = sb("br_hi", [P, NH, S], F32R)
        br_lo = sb("br_lo", [P, NH, S], F32R)
        g = sb("g", [P, S])
        prev = sb("prev", [P, S])
        stage1_end = cur[0]
        stage3 = cur[0]
        score_at = [P * i * (i + 1) // 2 for i in range(NT + 1)]
        score = sb("score", [P, score_at[NT]])
        o_t = sb("o_t", [P, NH, S])
        unit = cur[0]

        cur[0] = stage1
        mem_hi = sb("mem_hi", [P, KT, M], F32R)
        mem_lo = sb("mem_lo", [P, KT, M], F32R)
        qi_t = sb("qi_t", [P, 4, S])
        ki_t = sb("ki_t", [P, 2, S])
        assert cur[0] <= stage1_end
        cur[0] = unit
        relu = [sb(f"relu{i}", [P, S]) for i in range(2)]
        kx, sqk, vtc = sb("kx", [P, M]), sb("sqk", [P, M]), sb("vtc", [P, M])
        vc_n = sb("vc_n", [P, NTM, P])
        qx, sqq, zc = sb("qx", [P, S]), sb("sqq", [P, S]), sb("zc", [P, S])
        pc = [sb(f"pc{i}", [P, CH, M]) for i in range(2)]
        ptc = [sb(f"ptc{i}", [P, NTM, HALF]) for i in range(2)]
        xt, tmp = [relu[0], relu[1], qx, sqq], pc
        kiwi, rows, junk, dup = ptc[0], ptc[1], zc, vtc
        diag = [kx[:, i * P:(i + 1) * P] for i in range(2)]
        ends = [cur[0]]
        cur[0] = unit
        bq, bk, bb, bz = (sb(n, [P, S]) for n in ("bq", "bk", "bb", "bz"))
        bvn = sb("bvn", [P, NT, P])
        bvt = sb("bvt", [P, NT, P])
        bf = [sb(f"bf{i}", [P, HALF]) for i in range(2)]
        bm = [sb(f"bm{i}", [P, HALF]) for i in range(2)]
        bs, bqe, bkd, bkn = (sb(n, [P, HALF]) for n in ("bs", "bqe", "bkd", "bkn"))
        lmask = sb("lmask", [P, NL, P], BF16)
        ends.append(cur[0])
        cur[0] = unit
        q_aug, k_aug = sb("q_aug", [P, 2, S]), sb("k_aug", [P, 2, S])
        va = sb("va", [P, NT, 192])
        az = sb("az", [P, S])
        ta = [sb(f"ta{i}", [P, S]) for i in range(4)]
        rc, on = sb("rc", [P, P]), sb("on", [P, P])
        ends.append(cur[0])
        cur[0] = stage3
        m_hi, m_lo = sb("m_hi", [P, KT, S], F32R), sb("m_lo", [P, KT, S], F32R)
        ends.append(cur[0])
        cur[0] = h_lo_at
        xr = sb("xr", [P, 2 * NT, HALF])
        assert max(ends) <= nc.sbuf_usable_end, (ends, nc.sbuf_usable_end)

        pj = [ctx.enter_context(nc.psum_tensor(f"pj{i}", [P, S], F32)) for i in range(2)]
        px = [ctx.enter_context(nc.psum_tensor(f"px{i}", [P, S], F32)) for i in range(2)]

        g_in, g_mem = pcol[:, 0:8], pcol[:, 8:16]
        g_o, g_kc, g_ka = pcol[:, 24:25], pcol[:, 26:27], pcol[:, 28:29]
        g_qc, g_qa = pcol[:, 29:30], pcol[:, 30:31]
        lb, oml, neg_oml = lbt[:, 3, :], lbt[:, 4, :], lbt[:, 5, :]

        def freed(n):
            a = USES[n][0] in ACT_LAST
            n = sum((u[0] in ACT_LAST) == a and u[0] != "wo" for u in USES[:n + 1])
            return (sem("slot_read_act" if a else "slot_read_dve"), n)

        def read(kind, n):
            return freed(SLOT[(kind, n)])

        def tanh_done(n):
            return (sem("tanh"), sum(u[0] in GATED for u in USES[:n + 1]))

        def halves(n):
            return [slice(c, min(c + HALF, n)) for c in range(0, n, HALF)]

        def score_tile(i):
            return score[:, score_at[i]:score_at[i + 1]]

        def index_no(i, h):
            return IDX_TILES.index(i) * IDX_HEADS + h

        def store(sp, t):
            nh, m = divmod(t, NT)
            sp.wait_ge(sem("y_sum"), t + 1)
            sp.dma_start(out_t[m][:, nh * HALF:(nh + 1) * HALF], xr[:, t, :]).then_inc(sem("y_out"), 16)

        def product_no(n):
            return n // NL * (NL + 1) + 1 + n % NL

        def by_tile(t):
            return t[:].rearrange("p a (b t) -> p (a b) t", t=P)

        def y_bank(m):
            return (px + pj)[m // 2][:, m % 2 * HALF:(m % 2 + 1) * HALF]

        block = ctx.enter_context(nc.Block())

        @block.sync
        def _(sp):
            def load(j):
                if j >= 2:
                    sp.wait_ge(sem("w_lo"), j - 1)
                w = weights(j)
                dst = raw[:, j % 2, 0:w.shape[1] * w.shape[2]].rearrange("p (k n) -> p k n", k=w.shape[1])
                sp.dma_start(dst, w).then_inc(sem(f"raw_in{j % 2}"), 16)

            for a in range(ROWS_AHEAD):
                src = x_t[a]
                sp.dma_start(xt[a][:], src).then_inc(sem(f"x_in{a}"), 16)
            lb2 = lower_bounds.rearrange("l (h p) -> (l h) p", p=P)
            for r0, r1, src in ((0, 8, norm_in[0].rearrange("(k p) -> k p", p=P)),
                                (8, 16, norm_mem[0].rearrange("(k p) -> k p", p=P)),
                                (16, 24, lb2), (24, 25, o_norm_b), (25, 26, q_norm_c), (26, 27, k_norm_c)):
                sp.dma_start(rows[r0:r1, 0, 0:P], src).then_inc(sem("params_in"), 16)
            for r, src in ((27, q_norm_a), (28, k_norm_a)):
                for e in range(2):
                    sp.dma_start(rows[r:r + 1, 0, 64 * e:64 * e + 64], src).then_inc(sem("params_in"), 16)
            def rows_in(a):
                if a >= ROWS_AHEAD:
                    sp.wait_ge(sem("h_turned"), a - ROWS_AHEAD + 1)
                src = x_t[a] if a < NT else mem_t[a - NT]
                sp.dma_start(xt[a % ROWS_AHEAD][:], src).then_inc(sem(f"x_in{a % ROWS_AHEAD}"), 16)

            load(0)
            load(1)
            for a in range(ROWS_AHEAD, NT + NTM):
                rows_in(a)
            for step in TL:
                if step[0] != "job":
                    continue
                kind, n = step[1:]
                j = JOB[(kind, n)]
                if j + 2 < NJ:
                    load(j + 2)
                if kind == "gate" and n[0] > 0:
                    r, d = n
                    sp.wait_ge(sem("merged_out"), 16 * KT * r)
                    if r * KT + d > KT:
                        sp.wait_ge(sem("merged_sum"), (r - 1) * KT + d)
                    sp.dma_start(prev[:], merged_t[d]).then_inc(sem("merged_in"), 16)
                if kind == "br" and n[0] < 2:
                    r, d = n
                    if r == 0:
                        sp.wait_ge(*read("br", n))
                    else:
                        sp.wait_ge(sem("merged_sum"), (r - 1) * KT + d + 1)
                    sp.dma_start(merged_t[d], g[:]).then_inc(sem("merged_out"), 16)
                if kind == "wo":
                    if n == (0, 0):
                        sp.wait_ge(sem("proj_done"), JOB[("gate", (2, KT - 1))] + 1)
                        for nh in range(2):
                            src = x[0].rearrange("(t p) (h d) -> h p t d", p=P, h=2)[nh]
                            sp.dma_start(xr[:, nh * NT:(nh + 1) * NT, :], src).then_inc(sem(f"res_in{nh}"), 16)
            for t in range(2 * NT):
                store(sp, t)
            sp.wait_ge(sem("y_out"), 16 * 2 * NT)
            sp.wait_ge(sem("merged_out"), 16 * KT * 2)

        @block.gpsimd
        def _(pool):
            chain = [0]

            def link(ins):
                chain[0] += 1
                ins.then_inc(sem("pool_chain"), 1)
                pool.wait_ge(sem("pool_chain"), chain[0])

            def lo(j):
                pool.wait_ge(sem("w_hi"), j + 1)
                n = weights(j).shape[1] * weights(j).shape[2]
                s = j % 2
                pool.tensor_tensor(w_lo[:, s, 0:n], raw[:, s, 0:n], w_hi[:, s, 0:n].bitcast(F32),
                                   ALU.subtract).then_inc(sem("w_lo"), 1)

            link(pool.memset(ident[:], 0.0))
            pool.affine_select(out=ident[:], in_=ident[:], compare_op=ALU.not_equal, fill=1.0, base=0,
                               pattern=[[-1, P]], channel_multiplier=1).then_inc(sem("ident"), 1)
            pool.wait_ge(sem("ident"), 1)
            link(pool.memset(eps[:], EPS))
            link(pool.memset(ones_mean[:], 1.0 / P))
            link(pool.memset(ones_scan[:], 1.0))
            link(pool.memset(ones_mean_a[:], 0.0))
            link(pool.memset(ones_mean_a[0:64, 0:64], 1.0 / 64))
            pool.memset(ones_mean_a[64:128, 64:128], 1.0 / 64).then_inc(sem("consts"), 1)
            pool.wait_ge(sem("consts"), 1)
            link(pool.tensor_copy(dup[0:64, 0:64], ident[0:64, 0:64]))
            link(pool.tensor_copy(dup[0:64, 64:128], ident[0:64, 0:64]))
            link(pool.memset(ki_t[64:128, 0, :], 0.0))
            pool.memset(ki_t[0:64, 1, :], 0.0).then_inc(sem("index_consts"), 1)
            pool.wait_ge(sem("index_consts"), 1)
            for i in range(IDX_TILES[0]):
                link(pool.memset(score_tile(i), 0.0))
                diag = score_tile(i)[:, i * P:(i + 1) * P]
                pool.affine_select(out=diag, in_=diag, compare_op=ALU.is_ge, fill=BIG, base=0,
                                   pattern=[[-1, P]], channel_multiplier=1).then_inc(sem("causal_mask"), 1)
            lo(0)
            lo(1)
            for l, m in enumerate(LEVELS):
                nb = P // (2 * m)
                link(pool.memset(lmask[:, l, :], 0.0))
                v = lmask[:, l, :].rearrange("p (n two m) -> p n two m", two=2, m=m)[:, :, 1, :]
                link(pool.memset(v, 1.0))
                link(pool.affine_select(out=v, in_=v, compare_op=ALU.is_ge, fill=0.0, base=0,
                                        pattern=[[-2 * m, nb], [0, m]], channel_multiplier=1))
                last = pool.affine_select(out=v, in_=v, compare_op=ALU.is_ge, fill=0.0, base=m - 1,
                                          pattern=[[2 * m, nb], [0, m]], channel_multiplier=-1)
                last.then_inc(sem("level_masks"), 1)

            def index(i, h):
                if h < IDX_HEADS - 1:
                    return
                pool.wait_ge(sem("index_sum"), index_no(i, IDX_HEADS - 1) + 1)
                diag = score_tile(i)[:, i * P:(i + 1) * P]
                pool.affine_select(out=diag, in_=diag, compare_op=ALU.is_ge, fill=NONCAUSAL, base=0,
                                   pattern=[[-1, P]], channel_multiplier=1).then_inc(sem("index_causal"), 1)

            def memory(h, part):
                for hf in range(2) if part == 1 else ():
                    hh = 2 * h + hf
                    pool.wait_ge(sem("c_recip"), hh + 1)
                    r = small[:, 8 + 4 * hf:12 + 4 * hf].unsqueeze(2).broadcast_to([P, CH, M])
                    pool.tensor_tensor(pc[hf][:], pc[hf][:], r, ALU.mult).then_inc(sem("c_normed"), 1)

            def split(r, h):
                pool.wait_ge(sem("split_hi"), r * NH + h + 1)
                pool.tensor_tensor(br_lo[:, h, :], o_t[:, h, :], br_hi[:, h, :].bitcast(F32),
                                   ALU.subtract).then_inc(sem("split_lo"), 1)

            def recur(h, part):
                hf, part = divmod(part, REC_PARTS)
                hh = 2 * h + hf
                c0 = hf * HALF
                if part == 0:
                    pool.wait_ge(*read("qb", h))
                    pool.wait_ge(sem("b_keys"), h + 1)
                    pool.wait_ge(sem("b_kdecay"), hh + 1)
                    pool.tensor_tensor(bkd[:], bkd[:], bk[:, c0:c0 + HALF], ALU.mult).then_inc(sem("b_kmul"), 1)
                if part == REC_PARTS - 2:
                    pool.wait_ge(sem("b_qdecay"), hh + 1)
                    pool.tensor_tensor(bqe[:], bqe[:], bq[:, c0:c0 + HALF], ALU.mult).then_inc(sem("b_qmul"), 1)
                for l in REC_LEVELS[part]:
                    m = LEVELS[l]
                    n = hh * NL + l
                    pool.wait_ge(sem("b_exp"), n + 1)
                    if n >= 2:
                        pool.wait_ge(sem("b_product"), product_no(n - 2) + 1)
                    f = bf[n % 2][:].rearrange("p (n two m) -> p n two m", two=2, m=m)
                    o = bm[n % 2][:].rearrange("p (n two m) -> p n two m", two=2, m=m)
                    for side, src in ((0, bk), (1, bq)):
                        v = src[:, c0:c0 + HALF].rearrange("p (n two m) -> p n two m", two=2, m=m)
                        last = pool.tensor_tensor(o[:, :, side, :], f[:, :, side, :], v[:, :, side, :], ALU.mult)
                    last.then_inc(sem("b_mul"), 1)

            def positions():
                pool.wait_ge(sem("alibi_cleared"), 1)
                pool.wait_ge(sem("w_lo"), JOB[("va", 0)] + 3)
                link(pool.iota(q_aug[96:97, :, :], pattern=[[0, 2], [1, S]], base=0, channel_multiplier=0,
                               allow_small_or_imprecise_dtypes=True))
                pool.iota(k_aug[64:65, :, :], pattern=[[0, 2], [1, S]], base=0, channel_multiplier=0,
                          allow_small_or_imprecise_dtypes=True).then_inc(sem("positions"), 1)
                pool.wait_ge(sem("positions"), 1)

            for step in TL:
                if step[0] == "job":
                    kind, n = step[1:]
                    j = JOB[(kind, n)]
                    if j + 2 < NJ:
                        lo(j + 2)
                    if kind == "br" and n[0] == 2:
                        pool.wait_ge(sem("merged_hi"), n[1] + 1)
                        pool.tensor_tensor(m_lo[:, n[1], :], g[:], m_hi[:, n[1], :].bitcast(F32),
                                           ALU.subtract).then_inc(sem("merged_lo"), 1)
                elif step[0] == "index":
                    index(*step[1:])
                elif step[0] == "memory":
                    memory(*step[1:])
                elif step[0] == "split":
                    split(*step[1:])
                elif step[0] == "recur":
                    recur(*step[1:])
                elif step[0] == "positions":
                    positions()

        @block.scalar
        def _(act):
            chain = [0]

            def link(ins):
                chain[0] += 1
                ins.then_inc(sem("act_chain"), 1)
                act.wait_ge(sem("act_chain"), chain[0])

            def hi(j):
                act.wait_ge(sem(f"raw_in{j % 2}"), 16 * (j // 2 + 1))
                if j >= 2:
                    act.wait_ge(sem("proj_done"), j - 1)
                n = weights(j).shape[1] * weights(j).shape[2]
                act.activation(w_hi[:, j % 2, 0:n], raw[:, j % 2, 0:n], ACT.Copy).then_inc(sem("w_hi"), 1)

            def ln_and_exp():
                nc.scalar.preload_act_table_set("natural_log_exp_and_others")

            def rsqrt(dst, src, scale=1.0):
                link(act.activation(dst, src, ACT.Ln, bias=eps[0:dst.shape[0], :], scale=scale))
                return act.activation(dst, dst, ACT.Exp, scale=-0.5)

            def rms(a):
                act.wait_ge(sem(f"x_in{a % ROWS_AHEAD}"), 16 * (a // ROWS_AHEAD + 1))
                link(act.activation(junk[:], xt[a % ROWS_AHEAD][:], ACT.Square, accum_out=ssq[:, a:a + 1]))
                rsqrt(ssq[:, a:a + 1], ssq[:, a:a + 1], 1.0 / D).then_inc(sem("h_rms"), 1)

            ln_and_exp()
            act.wait_ge(sem("consts"), 1)
            rms(0)
            act.wait_ge(sem("params_turned"), 1)
            act.activation(pcol[:, 0:29], px[0][:, 0:29], ACT.Copy).then_inc(sem("params"), 1)
            rms(1)
            act.wait_ge(sem("lb_shifted"), 1)
            act.activation(lbt[:, 1:3, :], lbt[:, 1:3, :], ACT.Exp).then_inc(sem("lb_exp"), 1)
            hi(0)
            hi(1)

            def rows_step(a):
                if a + 2 < NT + NTM:
                    rms(a + 2)
                act.wait_ge(sem("h_gained"), a + 1)
                dst = h_hi[:, :, a * P:(a + 1) * P] if a < NT else mem_hi[:, :, (a - NT) * P:(a - NT + 1) * P]
                act.activation(dst, by_tile(tmp[a % 2]), ACT.Copy).then_inc(sem("h_hi"), 1)

            def spread():
                act.wait_ge(sem("index_consts"), 1)
                act.wait_ge(sem("ki_spread"), 1)
                act.activation(ki_t[0:64, 0, :], px[0][0:64, :], ACT.Copy)
                act.activation(ki_t[64:128, 1, :], px[0][64:128, :], ACT.Copy)
                v = px[1][:].rearrange("p (t c) -> p t c", c=P)[:, :, IDX_DIM:N_KIWI]
                act.activation(wn[:], v, ACT.Copy, scale=IDX_SCALE).then_inc(sem("index_in"), 1)

            def index(i, h):
                q, u = index_no(i, h), SLOT[("index", i, h)]
                act.wait_ge(sem("index_rel"), q + 1)
                if q >= 2:
                    act.wait_ge(sem("index_sum"), q - 1)
                w = (i + 1) * P
                act.activation(relu[q % 2][:, 0:w], pj[u % 2][:, 0:w], ACT.Relu).then_inc(sem("slot_read_act"), 1)

            def memory(h, part):
                if part == 0:
                    act.wait_ge(sem("c_kmean"), h + 1)
                    act.activation(vc_n[:].rearrange("p a b -> p (a b)"), px[0][:, HALF:HALF + M], ACT.Copy)
                    act.activation(sqk[:], px[0][:, 0:M], ACT.Ln, bias=eps[:])
                    act.wait_ge(sem("c_qmean"), h + 1)
                    link(act.activation(sqq[:], px[1][:], ACT.Ln, bias=eps[:]))
                    act.activation(sqk[:], sqk[:], ACT.Exp, scale=-0.5).then_inc(sem("c_krms"), 1)
                    act.activation(sqq[:], sqq[:], ACT.Exp, scale=-0.5).then_inc(sem("c_qrms"), 1)
                for hf in range(2) if part == 1 else ():
                    hh = 2 * h + hf
                    act.wait_ge(sem("c_max"), hh + 1)
                    for c in range(CH):
                        last = act.activation(pc[hf][:, c, :], px[hf][:, c * M:(c + 1) * M], ACT.Exp, scale=-1.0,
                                              bias=small[:, 4 * hf + c:4 * hf + c + 1],
                                              accum_out=small[:, 16 + 4 * hf + c:17 + 4 * hf + c])
                    last.then_inc(sem("c_exp"), 1)
                for hf in range(2) if part == 2 else ():
                    act.wait_ge(sem("c_pturned"), 2 * h + hf + 1)
                    act.activation(ptc[hf][:].rearrange("p a b -> p (a b)"), px[hf][:], ACT.Copy).then_inc(sem("c_pt"), 1)

            def split(r, h):
                name, per = {0: ("c_out", 2), 1: ("b_out", 2), 2: ("a_out", 16)}[r]
                if r > 0:
                    act.wait_ge(sem("proj_done"), LAST_BR[r - 1] + 1)
                act.wait_ge(sem(name), per * (h + 1))
                act.activation(br_hi[:, h, :], o_t[:, h, :], ACT.Copy).then_inc(sem("split_hi"), 1)

            def recur(h, part):
                hf, part = divmod(part, REC_PARTS)
                hh = 2 * h + hf
                c0 = hf * HALF
                if hf == 0 and part == 0:
                    act.wait_ge(sem("b_vturned"), h + 1)
                    act.activation(bvn[:].rearrange("p a b -> p (a b)"), px[1][:], ACT.Copy).then_inc(sem("b_values"), 1)
                if part == 0:
                    act.wait_ge(sem("b_kdiff"), hh + 1)
                    act.activation(bkd[:], bkd[:], ACT.Exp).then_inc(sem("b_kdecay"), 1)
                for l in REC_LEVELS[part]:
                    n = hh * NL + l
                    act.wait_ge(sem("b_diff"), n + 1)
                    act.activation(bf[n % 2][:], bf[n % 2][:], ACT.Exp).then_inc(sem("b_exp"), 1)
                if part == 1:
                    act.wait_ge(sem("b_kturned"), hh + 1)
                    act.activation(bkn[:], px[1][:, 0:HALF], ACT.Copy).then_inc(sem("b_kn"), 1)
                    if hf == 0:
                        last = bb[:].rearrange("p (c t) -> p c t", t=P)[:, :, P - 1]
                        act.activation(el[:], last, ACT.Exp).then_inc(sem("b_chunk_decay"), 1)
                if part == 2:
                    if hh:
                        act.wait_ge(sem("b_out"), hh)
                    act.activation(bqe[:], bb[:, c0:c0 + HALF], ACT.Exp).then_inc(sem("b_qdecay"), 1)
                if part == REC_PARTS - 1:
                    act.wait_ge(sem("b_o"), hh + 1)
                    act.activation(bkd[:], px[1][:, 0:HALF], ACT.Square, scale=0.5).then_inc(sem("b_square"), 1)
                    act.wait_ge(sem("b_mean"), hh + 1)
                    rsqrt(bkd[:], px[1][:, HALF:S]).then_inc(sem("b_rms"), 1)

            def keys(b):
                act.wait_ge(sem("a_kmean"), b + 1)
                ln_and_exp()
                rsqrt(ta[1][:], px[0][:]).then_inc(sem("a_krms"), 1)
                act.wait_ge(sem("a_vturned"), b + 1)
                dst = va[:].rearrange("p t (three c) -> p t three c", three=3)[:, :, 0:3:2, :]
                act.activation(dst, px[1][:].rearrange("p (t e c) -> p t e c", t=NT, e=2), ACT.Copy).then_inc(sem("a_values"), 1)

            def exps(b, u):
                w = (u % NT + 1) * P
                act.wait_ge(sem("a_max"), 16 * b + u + 1)
                act.activation(ta[u % 2][:, 0:w], ta[u % 2][:, 0:w], ACT.Exp, scale=-1.0,
                               bias=small[:, 24 + u % 2:25 + u % 2]).then_inc(sem("a_exp"), 1)

            def queries(b):
                act.wait_ge(sem("a_qmean"), b + 1)
                ln_and_exp()
                rsqrt(ta[1][:], px[0][:]).then_inc(sem("a_qrms"), 1)
                exps(b, 0)

            def attend(b, u):
                w = (u % NT + 1) * P
                act.wait_ge(sem("a_pturned"), 16 * b + u + 1)
                act.activation(ta[2 + u % 2][:, 0:w], px[u % 2][:, 0:w], ACT.Copy).then_inc(sem("a_pt"), 1)
                if u + 1 < 16:
                    exps(b, u + 1)

            def job(kind, n):
                j = JOB[(kind, n)]
                act.wait_ge(sem("proj_done"), j + 1)
                if j + 2 < NJ:
                    hi(j + 2)
                slot = pj[SLOT[(kind, n)] % 2]
                read = sem("slot_read_act")
                if kind == "kiwi":
                    act.activation(kiwi[0:N_KIWI].rearrange("p a b -> p (a b)"), slot[0:N_KIWI, :], ACT.Copy).then_inc(read, 1)
                elif kind == "qi":
                    act.activation(qi_t[:, n, :], slot[:], ACT.Copy).then_inc(read, 1)
                elif kind in ("kc", "vc", "qc", "zc"):
                    if n:
                        act.wait_ge(sem("c_out"), 2 * n)
                    if kind == "kc":
                        act.activation(kx[:], slot[:, 0:M], ACT.Copy)
                        act.activation(sqk[:], slot[:, 0:M], ACT.Square).then_inc(read, 1)
                    elif kind == "vc":
                        act.activation(vtc[:], slot[:, 0:M], ACT.Copy).then_inc(read, 1)
                    elif kind == "qc":
                        act.activation(qx[:], slot[:], ACT.Copy)
                        act.activation(sqq[:], slot[:], ACT.Square).then_inc(read, 1)
                    else:
                        act.activation(zc[:], slot[:], ACT.Tanh, scale=0.5).then_inc(sem("tanh"), 1)
                elif kind in ("fb", "ib", "gb", "qb"):
                    if kind == "fb" and n:
                        act.wait_ge(sem("b_diff"), 2 * n * NL)
                    else:
                        act.wait_ge(sem("b_out") if n else sem("c_out"), 2 * n if n else 2 * NH)
                    if kind == "fb":
                        act.activation(bb[:], slot[:], ACT.Sigmoid).then_inc(read, 1)
                    elif kind == "ib":
                        act.activation(bvt[:].rearrange("p a b -> p (a b)"), slot[:], ACT.Copy).then_inc(read, 1)
                        act.wait_ge(sem("b_keys"), n + 1)
                        act.activation(bb[:], bb[:], ACT.Ln, scale=oml[:, n:n + 1], bias=lb[:, n:n + 1]).then_inc(sem("b_logf"), 1)
                    else:
                        act.activation((bz if kind == "gb" else bq)[:], slot[:], ACT.Tanh, scale=0.5).then_inc(sem("tanh"), 1)
                elif kind in ("ka", "va", "qa", "za"):
                    act.wait_ge(sem("a_out") if n else sem("b_out"), 16 * n if n else 2 * NH)
                    if kind == "ka":
                        act.activation(ta[0][:], slot[:], ACT.Copy)
                        act.activation(ta[1][:], slot[:], ACT.Square).then_inc(read, 1)
                    elif kind == "va":
                        act.activation(ta[2][:], slot[:], ACT.Copy).then_inc(read, 1)
                    elif kind == "qa":
                        act.wait_ge(sem("a_keys"), n + 1)
                        act.activation(ta[3][:], slot[:], ACT.Copy)
                        act.activation(ta[1][:], slot[:], ACT.Square).then_inc(read, 1)
                    else:
                        act.activation(az[:], slot[:], ACT.Tanh, scale=0.5).then_inc(sem("tanh"), 1)
                elif kind == "gate":
                    r, d = n
                    t = r * KT + d
                    if 0 < t <= 2 * KT:
                        act.wait_ge(sem("merged_out"), 16 * t)
                    elif t:
                        act.wait_ge(sem("merged_lo"), d)
                    act.activation(g[:], slot[:], ACT.Tanh, scale=0.5).then_inc(read, 1)
                elif kind == "br" and n[0] == 2:
                    act.wait_ge(sem("merged_sum"), KT + n[1] + 1)
                    if n[1] == 0:
                        act.wait_ge(sem("split_lo"), 12)
                    act.activation(m_hi[:, n[1], :], g[:], ACT.Copy).then_inc(sem("merged_hi"), 1)

            for step in TL:
                if step[0] == "job":
                    job(*step[1:])
                elif step[0] == "rows":
                    rows_step(step[1])
                elif step[0] == "spread":
                    spread()
                elif step[0] == "index":
                    index(*step[1:])
                elif step[0] == "memory":
                    memory(*step[1:])
                elif step[0] == "queries":
                    queries(step[1])
                elif step[0] == "split":
                    split(*step[1:])
                elif step[0] == "recur":
                    recur(*step[1:])
                elif step[0] == "keys":
                    keys(step[1])
                elif step[0] == "attend":
                    attend(*step[1:])

        @block.vector
        def _(dve):
            chain = [0]

            def link(ins):
                chain[0] += 1
                ins.then_inc(sem("dve_chain"), 1)
                dve.wait_ge(sem("dve_chain"), chain[0])

            def scale(a):
                dve.wait_ge(sem("h_rms"), a + 1)
                if a >= 2:
                    dve.wait_ge(sem("h_turned"), a - 1)
                dve.tensor_scalar(diag[a % 2], ident[:], ssq[:, a:a + 1], None, ALU.mult).then_inc(sem("h_scaled"), 1)

            def low_part(a):
                dve.wait_ge(sem("h_hi"), a + 1)
                if a < NT:
                    t_hi, t_lo = (t[:, :, a * P:(a + 1) * P] for t in (h_hi, h_lo))
                else:
                    t_hi, t_lo = (t[:, :, (a - NT) * P:(a - NT + 1) * P] for t in (mem_hi, mem_lo))
                dve.tensor_tensor(t_lo, by_tile(tmp[a % 2]), t_hi.bitcast(F32), ALU.subtract).then_inc(sem("h_lo"), 1)

            def rows_step(a):
                if a + 1 < NT + NTM:
                    scale(a + 1)
                dve.wait_ge(sem("h_turned"), a + 1)
                if a >= 2:
                    dve.wait_ge(sem("h_lo"), a - 1)
                gain = g_in if a < NT else g_mem
                dve.tensor_tensor(by_tile(tmp[a % 2]), px[a % 2][:].rearrange("p (k t) -> p k t", k=KT),
                                  gain.unsqueeze(2).broadcast_to([P, KT, P]), ALU.mult).then_inc(sem("h_gained"), 1)
                if a not in (0, NT):
                    low_part(a - 1)
                if a in (NT - 1, NT + NTM - 1):
                    low_part(a)

            scale(0)

            dve.wait_ge(sem("params"), 1)
            link(dve.tensor_tensor(lbt[:, 0, :], pcol[:, 16:20], pcol[:, 20:24], ALU.max))
            dve.tensor_tensor(lbt[:, 1, :], pcol[:, 16:20], lbt[:, 0, :], ALU.subtract)
            dve.tensor_tensor(lbt[:, 2, :], pcol[:, 20:24], lbt[:, 0, :], ALU.subtract).then_inc(sem("lb_shifted"), 1)
            dve.tensor_scalar(g_qc, pcol[:, 25:26], -SCALE_C, None, ALU.mult)
            dve.tensor_scalar(g_qa, pcol[:, 27:28], -SCALE_A, None, ALU.mult)
            dve.wait_ge(sem("lb_exp"), 1)
            link(dve.tensor_tensor(lbt[:, 0, :], lbt[:, 1, :], lbt[:, 2, :], ALU.add))
            link(dve.reciprocal(lbt[:, 2, :], lbt[:, 0, :]))
            link(dve.tensor_tensor(lb, lbt[:, 1, :], lbt[:, 2, :], ALU.mult))
            link(dve.tensor_scalar(oml, lb, -1.0, 1.0, ALU.mult, ALU.add))
            link(dve.tensor_scalar(neg_oml, oml, -1.0, None, ALU.mult))

            def index(i, h):
                sc = score_tile(i)
                q = index_no(i, h)
                dve.wait_ge(*freed(SLOT[("index", i, h)]))
                r, w = relu[q % 2][:, 0:(i + 1) * P], wn[:, i, h:h + 1]
                if h == 0:
                    dve.tensor_scalar(sc, r, w, None, ALU.mult).then_inc(sem("index_sum"), 1)
                else:
                    dve.wait_ge(sem("index_sum"), q)
                    dve.scalar_tensor_tensor(out=sc, in0=r, scalar=w, in1=sc, op0=ALU.mult,
                                             op1=ALU.add).then_inc(sem("index_sum"), 1)

            done = [0]
            owed = [0]

            def topk(blocks, upto=NT):
                owed[0] += blocks
                while owed[0] > 0:
                    i, r = divmod(done[0], ROUNDS)
                    if i >= len(IDX_TILES) or IDX_TILES[i] >= upto:
                        owed[0] = 0
                        return
                    owed[0] -= IDX_TILES[i] + 1
                    sc = score_tile(IDX_TILES[i])
                    if r == 0:
                        dve.wait_ge(sem("index_causal"), i + 1)
                    link(dve.max(m8[:], sc))
                    link(dve.match_replace(sc, m8[:], sc, TAKEN))
                    if r == ROUNDS - 1:
                        link(dve.tensor_scalar(sc, sc, 0.99 * TAKEN, BIG, ALU.is_gt, ALU.mult))
                    done[0] += 1

            def memory(h, part):
                if part == 0:
                    dve.wait_ge(sem("c_krms"), h + 1)
                    dve.scalar_tensor_tensor(out=kx[:], in0=kx[:], scalar=g_kc, in1=sqk[:], op0=ALU.mult, op1=ALU.mult)
                    dve.wait_ge(sem("c_qrms"), h + 1)
                    dve.scalar_tensor_tensor(out=qx[:], in0=qx[:], scalar=g_qc, in1=sqq[:], op0=ALU.mult,
                                             op1=ALU.mult).then_inc(sem("c_qk"), 1)
                for hf in range(2) if part == 1 else ():
                    dve.wait_ge(sem("c_logits"), 2 * h + hf + 1)
                    dve.tensor_reduce(small[:, 4 * hf:4 * hf + 4], px[hf][:].rearrange("p (c m) -> p c m", m=M),
                                      AX_X, ALU.min).then_inc(sem("c_max"), 1)
                for hf in range(2) if part == 1 else ():
                    dve.wait_ge(sem("c_exp"), 2 * h + hf + 1)
                    dve.reciprocal(small[:, 8 + 4 * hf:12 + 4 * hf], small[:, 16 + 4 * hf:20 + 4 * hf]).then_inc(sem("c_recip"), 1)
                for hf in range(2) if part == 3 else ():
                    c0 = hf * HALF
                    dve.wait_ge(sem("c_o"), 2 * h + hf + 1)
                    dve.scalar_tensor_tensor(out=o_t[:, h, c0:c0 + HALF], in0=px[hf][:, 0:HALF], scalar=0.5,
                                             in1=zc[:, c0:c0 + HALF], op0=ALU.mult, op1=ALU.mult).then_inc(sem("c_out"), 1)

                topk(TOPK_MEMORY[part], next_index)

            def diffs(hh, l):
                n = hh * NL + l
                m = LEVELS[l]
                c0 = hh % 2 * HALF
                if n >= 2:
                    dve.wait_ge(sem("b_mul"), n - 1)
                v = bb[:, c0:c0 + HALF].rearrange("p (n two m) -> p n two m", two=2, m=m)
                f = bf[n % 2][:].rearrange("p (n two m) -> p n two m", two=2, m=m)
                mid = v[:, :, 0, m - 1:m].broadcast_to([P, HALF // (2 * m), m])
                dve.tensor_tensor(f[:, :, 0, :], mid, v[:, :, 0, :], ALU.subtract)
                dve.tensor_tensor(f[:, :, 1, :], v[:, :, 1, :], mid, ALU.subtract).then_inc(sem("b_diff"), 1)

            def gather(hh, l):
                p = hh * (NL + 1) + 1 + l
                dve.wait_ge(sem("b_product"), p + 1)
                src = px[0][:, p % 2 * HALF:(p % 2 + 1) * HALF].rearrange("p (c t) -> p c t", t=P)
                dst = bs[:].rearrange("p (c t) -> p c t", t=P)
                if l < 0:
                    if hh == 0:
                        dve.wait_ge(sem("level_masks"), NL)
                    dve.tensor_tensor(dst, src, ident[:].unsqueeze(1).broadcast_to([P, CH, P]),
                                      ALU.mult).then_inc(sem("b_gather"), 1)
                else:
                    dve.wait_ge(sem("b_gather"), p)
                    mask = lmask[:, l, :].bitcast(U16).unsqueeze(1).broadcast_to([P, CH, P])
                    dve.copy_predicated(dst, mask, src).then_inc(sem("b_gather"), 1)

            def states(h, hf):
                dve.wait_ge(sem("b_kv"), 2 * h + hf + 1)
                dve.wait_ge(sem("b_chunk_decay"), h + 1)
                for c in range(CH * hf, min(CH * hf + CH, NT - 1)):
                    kv = px[1][:, HALF + c % CH * P:HALF + (c % CH + 1) * P]
                    if c == 0:
                        dve.tensor_copy(bvt[:, 1, :], kv).then_inc(sem("b_state"), 1)
                    else:
                        dve.wait_ge(sem("b_state"), h * (NT - 1) + c)
                        dve.scalar_tensor_tensor(out=bvt[:, c + 1, :], in0=bvt[:, c, :], scalar=el[:, c:c + 1],
                                                 in1=kv, op0=ALU.mult, op1=ALU.add).then_inc(sem("b_state"), 1)

            def recur(h, part):
                hf, part = divmod(part, REC_PARTS)
                hh = 2 * h + hf
                c0 = hf * HALF
                if part == 0:
                    v = bb[:, c0:c0 + HALF].rearrange("p (c t) -> p c t", t=P)
                    dve.wait_ge(sem("b_cumsum"), h + 1)
                    if hh:
                        dve.wait_ge(sem("b_out"), hh)
                    dve.tensor_tensor(bkd[:].rearrange("p (c t) -> p c t", t=P),
                                      v[:, :, P - 1:P].broadcast_to([P, CH, P]), v, ALU.subtract).then_inc(sem("b_kdiff"), 1)
                    diffs(hh, 0)
                    diffs(hh, 1)
                    gather(hh, -1)
                for l in REC_LEVELS[part]:
                    if l + 2 < NL:
                        diffs(hh, l + 2)
                    gather(hh, l)
                    topk(TOPK_LEVEL[part])
                if part == 2:
                    states(h, hf)
                if part == REC_PARTS - 1:
                    dve.wait_ge(sem("b_rms"), hh + 1)
                    link(dve.scalar_tensor_tensor(out=bqe[:], in0=px[1][:, 0:HALF], scalar=g_o, in1=bkd[:],
                                                  op0=ALU.mult, op1=ALU.mult))
                    if hh == 0:
                        dve.wait_ge(sem("split_lo"), NH)
                    dve.scalar_tensor_tensor(out=o_t[:, h, c0:c0 + HALF], in0=bqe[:], scalar=0.25,
                                             in1=bz[:, c0:c0 + HALF], op0=ALU.mult, op1=ALU.mult).then_inc(sem("b_out"), 1)
                topk(TOPK_REC[part])

            def normed_heads(dst, src, gain, rms):
                for e in range(2):
                    p = slice(64 * e, 64 * e + 64)
                    last = dve.scalar_tensor_tensor(out=dst[0:64, e, :], in0=src[p, :], scalar=gain[p, :], in1=rms[p, :],
                                                    op0=ALU.mult, op1=ALU.mult)
                return last

            def keys(b):
                if b == 0:
                    dve.wait_ge(sem("positions"), 1)
                    for e in range(2):
                        link(dve.tensor_scalar(k_aug[64:65, e, :], k_aug[64:65, e, :], 2.0 ** -(e + 1), None, ALU.mult))
                else:
                    link(dve.tensor_scalar(k_aug[64:128, :, :], k_aug[64:128, :, :], 0.25, None, ALU.mult))
                dve.wait_ge(sem("a_krms"), b + 1)
                normed_heads(k_aug, ta[0], g_ka, ta[1]).then_inc(sem("a_keys"), 1)

            def alibi():
                for t in (q_aug, k_aug):
                    link(dve.memset(t[64:128, :, :], 0.0))
                dve.memset(q_aug[64:65, :, :], -1.0)
                for e in range(2):
                    dve.memset(k_aug[96:97, e, :], 2.0 ** -(e + 1))
                dve.memset(va[:, :, 64:128], 1.0).then_inc(sem("alibi_cleared"), 1)

            def mask(b, u):
                a, i = 16 * b + u, u % NT
                w = (i + 1) * P
                if b == 0 and i >= IDX_TILES[0]:
                    topk(10 ** 6, i + 1)
                if b == 0 and i < IDX_TILES[0]:
                    dve.wait_ge(sem("causal_mask"), i + 1)
                dve.wait_ge(sem("a_logits"), a + 1)
                dve.tensor_tensor_reduce(ta[u % 2][:, 0:w], px[u % 2][:, 0:w], score_tile(i), 1.0, 3e38, ALU.add,
                                         ALU.min, small[:, 24 + u % 2:25 + u % 2]).then_inc(sem("a_max"), 1)

            def queries(b):
                dve.wait_ge(sem("a_qrms"), b + 1)
                normed_heads(q_aug, ta[3], g_qa, ta[1]).then_inc(sem("a_queries"), 1)
                mask(b, 0)

            def attend(b, u):
                if u + 1 < 16:
                    mask(b, u + 1)
                e, i = divmod(u, NT)
                own, other = slice(64 * e, 64 * e + 64), slice(64 - 64 * e, 128 - 64 * e)
                dve.wait_ge(sem("a_o"), 16 * b + u + 1)
                link(dve.reciprocal(rc[own, :], px[u % 2][other, 0:P]))
                link(dve.tensor_tensor(on[own, :], px[u % 2][own, 0:P], rc[own, :], ALU.mult))
                if b == 0 and u == 0:
                    dve.wait_ge(sem("split_lo"), 2 * NH)
                dve.scalar_tensor_tensor(out=o_t[own, b, i * P:(i + 1) * P], in0=on[own, :], scalar=0.5,
                                         in1=az[own, i * P:(i + 1) * P], op0=ALU.mult, op1=ALU.mult).then_inc(sem("a_out"), 1)

            def job(kind, n):
                j = JOB[(kind, n)]
                slot = pj[SLOT[(kind, n)] % 2]
                if kind in GATED:
                    buf = {"zc": zc, "gb": bz, "qb": bq, "za": az}[kind]
                    dve.wait_ge(*tanh_done(SLOT[(kind, n)]))
                    dve.scalar_tensor_tensor(out=buf[:], in0=buf[:], scalar=1.0, in1=slot[:], op0=ALU.add,
                                             op1=ALU.mult).then_inc(sem("slot_read_dve"), 1)
                elif kind == "fb":
                    if n == 0:
                        topk(TOPK_DECAY)
                    dve.wait_ge(*read("fb", n))
                    dve.tensor_scalar(bk[:], bb[:], neg_oml[:, n:n + 1], oml[:, n:n + 1], ALU.mult,
                                      ALU.add).then_inc(sem("b_keys"), 1)
                elif kind == "ib":
                    dve.wait_ge(sem("b_logf"), n + 1)
                    for c in range(NT):
                        v = bb[:, c * P:(c + 1) * P]
                        last = dve.tensor_tensor_scan(v, ones_scan[:], v, 0.0, ALU.mult, ALU.add)
                    last.then_inc(sem("b_cumsum"), 1)
                elif kind == "br":
                    r, d = n
                    dve.wait_ge(sem("proj_done"), j + 1)
                    dve.wait_ge(*read("gate", n))
                    dve.scalar_tensor_tensor(out=g[:], in0=g[:], scalar=1.0, in1=slot[:], op0=ALU.add,
                                             op1=ALU.mult).then_inc(sem("slot_read_dve"), 1)
                    if r:
                        dve.wait_ge(*read("br", n))
                        dve.wait_ge(sem("merged_in"), 16 * ((r - 1) * KT + d + 1))
                        dve.tensor_tensor(g[:], g[:], prev[:], ALU.add).then_inc(sem("merged_sum"), 1)
                if kind in TOPK_JOB:
                    topk(TOPK_JOB[kind][min(n, 1)], next_index)

            next_index = IDX_TILES[0]
            for step in TL:
                if step[0] == "job":
                    if step[1] == "wo":
                        break
                    job(*step[1:])
                elif step[0] == "rows":
                    rows_step(step[1])
                elif step[0] == "index":
                    index(*step[1:])
                    next_index = step[1] + (step[2] == IDX_HEADS - 1)
                elif step[0] == "memory":
                    memory(*step[1:])
                elif step[0] == "recur":
                    recur(*step[1:])
                elif step[0] == "alibi":
                    alibi()
                elif step[0] == "queries":
                    queries(step[1])
                elif step[0] == "keys":
                    keys(step[1])
                elif step[0] == "attend":
                    attend(*step[1:])
                    topk(TOPK_ATT)
            for t in range(2 * NT):
                nh, m = divmod(t, NT)
                if m < NT - 1:
                    dve.wait_ge(sem("y_proj"), nh * (NT - 1) + m + 1)
                else:
                    dve.wait_ge(sem("proj_done"), WO0 + 4 * (nh + 1))
                dve.wait_ge(sem(f"res_in{nh}"), 16)
                dve.scalar_tensor_tensor(out=xr[:, t, :], in0=y_bank(m), scalar=0.5, in1=xr[:, t, :],
                                         op0=ALU.mult, op1=ALU.add).then_inc(sem("y_sum"), 1)

        @block.tensor
        def _(pe):
            def three(out, a_hi, a_lo, b_hi, b_lo, first, last):
                pe.matmul(out, a_hi, b_hi, start=first, stop=False)
                pe.matmul(out, a_hi, b_lo, start=False, stop=False)
                return pe.matmul(out, a_lo, b_hi, start=False, stop=last)

            pe.wait_ge(sem("ident"), 1)
            pe.wait_ge(sem("params_in"), 16 * 10)
            pe.transpose(px[0][:, 0:29], rows[0:29, 0, 0:P], ident[0:29, 0:29]).then_inc(sem("params_turned"), 1)
            def project(j, c):
                kind, n = JOBS[j]
                u, s = SLOT[(kind, n)], j % 2
                if c.start == 0:
                    pe.wait_ge(sem("w_lo"), j + 1)
                    if u >= 2:
                        pe.wait_ge(*freed(u - 2))
                hi, lo = h_hi, h_lo
                if kind in ("kc", "vc"):
                    hi, lo = mem_hi, mem_lo
                if kind == "br":
                    hi, lo = br_hi, br_lo
                if kind == "kc" and n == 0:
                    pe.wait_ge(sem("h_lo"), NT + NTM)
                kt, m = weights(j).shape[1:]
                if j == 0:
                    pe.wait_ge(sem("h_lo"), c.stop // P)
                for k in range(kt):
                    if kind == "br" and n[1] == 0 and c.start == 0:
                        pe.wait_ge(sem("split_lo"), NH * n[0] + k + 1)
                    last = three(pj[u % 2][0:m, c], w_hi[:, s, k * m:(k + 1) * m], w_lo[:, s, k * m:(k + 1) * m],
                                 hi[:, k, c], lo[:, k, c], k == 0, k == kt - 1)
                    if k == kt - 1 and c.stop == columns(j):
                        last.then_inc(sem("proj_done"), 1)
                    yield

            def columns(j):
                return M if JOBS[j][0] in ("kc", "vc") else S

            pieces = [(j, c, 1) for c in halves(S) for j in range(2)]
            pieces += [(j, c, j) for j in range(2, WO0) for c in halves(columns(j))]
            going = [None]

            def fill(n, last):
                while n and pieces and pieces[0][2] <= last:
                    if going[0] is None:
                        going[0] = project(*pieces[0][:2])
                    if next(going[0], "end") == "end":
                        going[0] = None
                        pieces.pop(0)
                    else:
                        n -= 1

            def rows_step(a):
                pe.wait_ge(sem("h_scaled"), a + 1)
                if a == 0:
                    pe.wait_ge(sem("params"), 1)
                if a >= 2:
                    pe.wait_ge(sem("h_gained"), a - 1)
                for k in range(KT):
                    last = pe.matmul(px[a % 2][:, k * P:(k + 1) * P], xt[a % ROWS_AHEAD][:, k * P:(k + 1) * P],
                                     diag[a % 2], start=True, stop=True)
                last.then_inc(sem("h_turned"), 1)
                if NT // 2 <= a < NT:
                    fill(FILL["rows"], 1)

            passed = [0]

            def meanwhile(n):
                nxt = USES[len(passed_uses):len(passed_uses) + 2]
                ahead = 0
                for use in nxt:
                    if use[0] in ("index", "wo") or (use[0] == "br" and not branch_ready(use[1][0])) or use[0] == "kc":
                        break
                    ahead += 1
                fill(n, passed[0] + ahead - 1)

            passed_uses = []
            splits_seen = [0]

            def branch_ready(r):
                return splits_seen[0] > r

            def job(kind, n):
                j = JOB[(kind, n)]
                if kind == "wo":
                    pe.wait_ge(sem("w_lo"), j + 1)
                    output(*n)
                else:
                    fill(-1, max(j, 1))
                passed[0] += 1
                passed_uses.append((kind, n))

            def output(nh, kk):
                s = (WO0 + nh * 4 + kk) % 2
                if nh == 0:
                    pe.wait_ge(sem("merged_lo"), 2 * kk + 2)
                for m in range(NT):
                    if nh == 0 and kk == 0 and m in (NT // 2, 3 * NT // 4):
                        pe.wait_ge(*freed(SLOT[JOBS[WO0]] - (1 if SLOT[JOBS[WO0 - 1]] % 2 == (m - NT // 2) // 2 else 2)))
                    if nh and kk == 0:
                        pe.wait_ge(sem("y_sum"), m + 1)
                    t = slice(m * P, (m + 1) * P)
                    for k2 in range(2):
                        k = 2 * kk + k2
                        c = slice(k2 * HALF, (k2 + 1) * HALF)
                        last = three(y_bank(m), m_hi[:, k, t], m_lo[:, k, t], w_hi[:, s, c], w_lo[:, s, c],
                                     k == 0, k == KT - 1)
                    if kk == 3 and m < NT - 1:
                        last.then_inc(sem("y_proj"), 1)
                last.then_inc(sem("proj_done"), 1)

            def spread():
                pe.wait_ge(*read("kiwi", 0))
                pe.wait_ge(sem("index_consts"), 1)
                pe.wait_ge(sem("h_gained"), NT + NTM)
                for c in range(2):
                    pe.matmul(px[0][:, c * HALF:(c + 1) * HALF], dup[0:64, 0:P], kiwi[0:64, c, :], start=True, stop=True)
                kf = kiwi[:].rearrange("p a b -> p (a b)")
                for i in range(NT):
                    last = pe.transpose(px[1][:, i * P:i * P + N_KIWI], kf[0:N_KIWI, i * P:(i + 1) * P],
                                        ident[0:N_KIWI, 0:N_KIWI])
                last.then_inc(sem("ki_spread"), 1)

            def index(i, h):
                u = SLOT[("index", i, h)]
                pe.wait_ge(*freed(u - 2))
                pe.wait_ge(sem("index_in"), 1)
                pe.wait_ge(*read("qi", 3))
                for c in halves((i + 1) * P):
                    last = pe.matmul(pj[u % 2][:, c], qi_t[:, h // 2, i * P:(i + 1) * P], ki_t[:, h % 2, c],
                                     start=True, stop=True)
                last.then_inc(sem("index_rel"), 1)
                passed_uses.append(("index", i, h))

            def memory(h, part):
                if part == 0:
                    pe.wait_ge(*read("vc", h))
                    if h:
                        pe.wait_ge(sem("c_out"), 2 * h)
                    pe.matmul(px[0][:, 0:M], ones_mean[:], sqk[:], start=True, stop=True)
                    for t in range(NTM):
                        last = pe.transpose(px[0][:, HALF + t * P:HALF + (t + 1) * P], vtc[:, t * P:(t + 1) * P], ident[:])
                    last.then_inc(sem("c_kmean"), 1)
                    pe.wait_ge(*read("qc", h))
                    for c in halves(S):
                        last = pe.matmul(px[1][:, c], ones_mean[:], sqq[:, c], start=True, stop=True)
                    last.then_inc(sem("c_qmean"), 1)
                for hf in range(2) if part == 1 else ():
                    pe.wait_ge(sem("c_qk"), h + 1)
                    for c in range(CH):
                        t = (hf * CH + c) * P
                        last = pe.matmul(px[hf][:, c * M:(c + 1) * M], qx[:, t:t + P], kx[:], start=True, stop=True)
                    last.then_inc(sem("c_logits"), 1)
                for hf in range(2) if part == 2 else ():
                    pe.wait_ge(sem("c_normed"), 2 * h + hf + 1)
                    for mb in range(NTM):
                        for c in range(CH):
                            last = pe.transpose(px[hf][:, mb * HALF + c * P:mb * HALF + (c + 1) * P],
                                                pc[hf][:, c, mb * P:(mb + 1) * P], ident[:])
                    last.then_inc(sem("c_pturned"), 1)
                for hf in range(2) if part == 3 else ():
                    pe.wait_ge(sem("c_pt"), 2 * h + hf + 1)
                    for mb in range(NTM):
                        last = pe.matmul(px[hf][:, 0:HALF], vc_n[:, mb, :], ptc[hf][:, mb, :], start=mb == 0, stop=mb == NTM - 1)
                    last.then_inc(sem("c_o"), 1)

            def products(hh, l):
                p = hh * (NL + 1) + 1 + l
                c0 = hh % 2 * HALF
                if p >= 2:
                    pe.wait_ge(sem("b_gather"), p - 1)
                if l >= 0:
                    pe.wait_ge(sem("b_mul"), hh * NL + l + 1)
                for c in range(CH):
                    o = px[0][:, p % 2 * HALF + c * P:p % 2 * HALF + (c + 1) * P]
                    if l < 0:
                        k, q = (t[:, c0 + c * P:c0 + (c + 1) * P] for t in (bk, bq))
                    else:
                        k = q = bm[(hh * NL + l) % 2][:, c * P:(c + 1) * P]
                    last = pe.matmul(o, k, q, start=True, stop=True)
                last.then_inc(sem("b_product"), 1)

            def recur(h, part):
                hf, part = divmod(part, REC_PARTS)
                hh = 2 * h + hf
                if hf == 0 and part == 0:
                    pe.wait_ge(*read("ib", h))
                    pe.wait_ge(sem("b_out") if h else sem("c_out"), 2 * h if h else 2 * NH)
                    for c in range(NT):
                        last = pe.transpose(px[1][:, c * P:(c + 1) * P], bvt[:, c, :], ident[:])
                    last.then_inc(sem("b_vturned"), 1)
                    pe.wait_ge(*read("qb", h))
                    pe.wait_ge(sem("b_keys"), h + 1)
                if part == 0:
                    products(hh, -1)
                for l in REC_LEVELS[part]:
                    meanwhile(FILL["level"])
                    products(hh, l)
                if part == 0:
                    meanwhile(FILL["keys"])
                    pe.wait_ge(sem("b_kmul"), hh + 1)
                    pe.wait_ge(sem("b_values"), h + 1)
                    if hh:
                        pe.wait_ge(sem("b_out"), hh)
                    for c in range(CH):
                        last = pe.transpose(px[1][:, c * P:(c + 1) * P], bkd[:, c * P:(c + 1) * P], ident[:])
                    last.then_inc(sem("b_kturned"), 1)
                if part == 1:
                    pe.wait_ge(sem("b_kn"), hh + 1)
                    for c in range(CH):
                        last = pe.matmul(px[1][:, HALF + c * P:HALF + (c + 1) * P], bkn[:, c * P:(c + 1) * P],
                                         bvn[:, hf * CH + c, :], start=True, stop=True)
                    last.then_inc(sem("b_kv"), 1)
                if part == REC_PARTS - 2:
                    meanwhile(FILL["output"])
                    pe.wait_ge(sem("b_gather"), (hh + 1) * (NL + 1))
                    pe.wait_ge(sem("b_qmul"), hh + 1)
                    for c in range(CH):
                        n = hf * CH + c
                        o = px[1][:, c * P:(c + 1) * P]
                        last = pe.matmul(o, bvn[:, n, :], bs[:, c * P:(c + 1) * P], start=True, stop=n == 0)
                        if n:
                            pe.wait_ge(sem("b_state"), h * (NT - 1) + n)
                            last = pe.matmul(o, bvt[:, n, :], bqe[:, c * P:(c + 1) * P], start=False, stop=True)
                    last.then_inc(sem("b_o"), 1)
                if part == REC_PARTS - 1:
                    meanwhile(FILL["square"])
                    pe.wait_ge(sem("b_square"), hh + 1)
                    pe.wait_ge(sem("b_state"), h * (NT - 1) + min(CH * hf + CH, NT - 1))
                    pe.matmul(px[1][:, HALF:S], ones_mean[:], bkd[:], start=True, stop=True).then_inc(sem("b_mean"), 1)
                    meanwhile(FILL["mean"])

            def keys(b):
                meanwhile(FILL["key"])
                pe.wait_ge(*read("ka", b))
                pe.wait_ge(sem("a_out") if b else sem("b_out"), 16 * b if b else 2 * NH)
                for c in halves(S):
                    last = pe.matmul(px[0][:, c], ones_mean_a[:], ta[1][:, c], start=True, stop=True)
                last.then_inc(sem("a_kmean"), 1)
                pe.wait_ge(*read("va", b))
                for i in range(NT):
                    last = pe.transpose(px[1][:, i * P:(i + 1) * P], ta[2][:, i * P:(i + 1) * P], ident[:])
                last.then_inc(sem("a_vturned"), 1)

            def logits(b, u):
                e, i = divmod(u, NT)
                if u >= 2:
                    pe.wait_ge(sem("a_out"), 16 * b + u - 1)
                for c in halves((i + 1) * P):
                    last = pe.matmul(px[u % 2][:, c], q_aug[:, e, i * P:(i + 1) * P], k_aug[:, e, c],
                                     start=True, stop=True)
                last.then_inc(sem("a_logits"), 1)

            def queries(b):
                meanwhile(FILL["qmean"])
                pe.wait_ge(*read("qa", b))
                pe.wait_ge(sem("a_krms"), b + 1)
                for c in halves(S):
                    last = pe.matmul(px[0][:, c], ones_mean_a[:], ta[1][:, c], start=True, stop=True)
                last.then_inc(sem("a_qmean"), 1)
                meanwhile(FILL["query"])
                pe.wait_ge(sem("a_queries"), b + 1)
                pe.wait_ge(sem("a_values"), b + 1)
                logits(b, 0)

            def attend(b, u):
                a = 16 * b + u
                e, i = divmod(u, NT)
                meanwhile(FILL["probs"])
                pe.wait_ge(sem("a_exp"), a + 1)
                for k in range(i + 1):
                    last = pe.transpose(px[u % 2][:, k * P:(k + 1) * P], ta[u % 2][:, k * P:(k + 1) * P], ident[:])
                last.then_inc(sem("a_pturned"), 1)
                if u + 1 < 16:
                    logits(b, u + 1)
                meanwhile(FILL["turned"])
                pe.wait_ge(sem("a_pt"), a + 1)
                for k in range(i + 1):
                    last = pe.matmul(px[u % 2][:, 0:P], va[:, k, 64 * e:64 * e + P], ta[2 + u % 2][:, k * P:(k + 1) * P],
                                     start=k == 0, stop=k == i)
                last.then_inc(sem("a_o"), 1)

            for step in TL:
                if step[0] == "job":
                    job(*step[1:])
                elif step[0] == "rows":
                    rows_step(step[1])
                elif step[0] == "spread":
                    spread()
                elif step[0] == "index":
                    index(*step[1:])
                elif step[0] == "memory":
                    memory(*step[1:])
                elif step[0] == "split":
                    splits_seen[0] += step[2] == NH - 1
                elif step[0] == "recur":
                    recur(*step[1:])
                elif step[0] == "keys":
                    keys(step[1])
                elif step[0] == "queries":
                    queries(step[1])
                elif step[0] == "attend":
                    attend(*step[1:])


_INS = ["x", "mem", "norm_in", "norm_mem", "w_in", "q_norm_a", "k_norm_a", "lower_bounds", "o_norm_b",
        "w_mem_kv", "q_norm_c", "k_norm_c", "w_branch", "w_out"]


def kernel(**inputs):
    import numpy as _np
    import concourse.bacc as _bacc
    from concourse.bass_utils import run_bass_kernel_spmd as _run

    nc = _bacc.Bacc("TRN2", target_bir_lowering=False, num_devices=1)
    arrays, args = {}, []
    for name in _INS:
        a = _np.ascontiguousarray(inputs[name])
        arrays[f"in_{name}"] = a
        args.append(nc.dram_tensor(f"in_{name}", a.shape, mybir.dt.from_np(a.dtype), kind="ExternalInput").ap())
    args.append(nc.dram_tensor("merged", [D, S], F32, kind="Internal").ap())
    args.append(nc.dram_tensor("out_0", [1, S, D], F32, kind="ExternalOutput").ap())
    hybrid_layer(nc, *args)
    r = _run(nc, [arrays], core_ids=[0])
    return r.results[0]["out_0"]
```
